# Optimizing a Trainium2 kernel written in Bass

```python
import math
import jax, jax.numpy as jnp
from jax import lax
import numpy as np

D_MODEL = 1024
BATCH = 1
SEQ = 1024
DEPTH = 1
DEC_BATCH = 1
DEC_SEQ = 64
PAST_LEN = 256

CHUNK = 64
Q_BLOCK = 128
MIX_WIDTH = D_MODEL
N_DIFF_HEADS = 4
DIFF_HEAD_DIM = 64
DIFF_WIDTH = N_DIFF_HEADS * 2 * DIFF_HEAD_DIM
N_DSA_HEADS = 8
N_DSA_KV_HEADS = 2
DSA_HEAD_DIM = 64
DSA_WIDTH = N_DSA_HEADS * DSA_HEAD_DIM
N_IDX_HEADS = 4
IDX_HEAD_DIM = 64
DSA_TOPK = 256
N_ATTN_HEADS = N_DIFF_HEADS + N_DSA_HEADS
NUM_BUCKETS = 32
MAX_DISTANCE = 256
D_FF = -(-8 * D_MODEL // (3 * 256)) * 256
IN_SIZES = (DIFF_WIDTH, DIFF_WIDTH, DIFF_WIDTH,
            DSA_WIDTH, N_DSA_KV_HEADS * DSA_HEAD_DIM, N_DSA_KV_HEADS * DSA_HEAD_DIM,
            N_IDX_HEADS * IDX_HEAD_DIM, IDX_HEAD_DIM, N_IDX_HEADS)
IN_WIDTH = sum(IN_SIZES)
RMS_EPS = 1e-6
NEG_INF = -1e30

kernel_name = "hymba_diffattn_dsa_streaming_step"

def rms_norm(x, g):
    xf = x.astype(jnp.float32)
    y = xf * lax.rsqrt(jnp.mean(xf * xf, axis=-1, keepdims=True) + RMS_EPS)
    return (y * g.astype(jnp.float32)).astype(x.dtype)

def rel_bucket(rel):
    nb = NUM_BUCKETS // 2
    max_exact = nb // 2
    ret = jnp.where(rel > 0, nb, 0)
    n = jnp.abs(rel)
    nf = jnp.maximum(n, 1).astype(jnp.float32)
    large = max_exact + (jnp.log(nf / max_exact) / math.log(MAX_DISTANCE / max_exact)
                         * (nb - max_exact)).astype(jnp.int32)
    large = jnp.minimum(large, nb - 1)
    return ret + jnp.where(n < max_exact, n, large)

def chunk_visible(qpos, kpos):
    return (kpos[None, :] // CHUNK) <= (qpos[:, None] // CHUNK)

def gather_rows(a, idx):
    return jax.vmap(lambda ab, ib: ab[ib])(a, idx)

def in_projection(h, w_in):
    B, T, _ = h.shape
    z = h @ w_in
    cuts, acc = [], 0
    for s in IN_SIZES[:-1]:
        acc += s
        cuts.append(acc)
    dq, dk, dv, sq, sk, sv, iq, ik, iw = jnp.split(z, cuts, axis=-1)
    hd = (B, T, N_DIFF_HEADS, 2 * DIFF_HEAD_DIM)
    return (dq.reshape(hd), dk.reshape(hd), dv.reshape(hd),
            sq.reshape(B, T, N_DSA_HEADS, DSA_HEAD_DIM),
            sk.reshape(B, T, N_DSA_KV_HEADS, DSA_HEAD_DIM),
            sv.reshape(B, T, N_DSA_KV_HEADS, DSA_HEAD_DIM),
            iq.reshape(B, T, N_IDX_HEADS, IDX_HEAD_DIM), ik, iw)

def diff_attn(q, k, v, qpos, kpos, lam, lam_init, g_subln, tab):
    f32 = jnp.float32
    dh = DIFF_HEAD_DIM
    qf = q.astype(f32) * (dh ** -0.5)
    kf = k.astype(f32)
    vis = chunk_visible(qpos, kpos)
    bias = jnp.transpose(tab.astype(f32)[rel_bucket(kpos[None, :] - qpos[:, None])], (2, 0, 1))

    def attn_map(qa, ka):
        s = jnp.einsum('bqhd,bkhd->bhqk', qa, ka) + bias[None]
        return jax.nn.softmax(jnp.where(vis, s, NEG_INF), axis=-1)

    a = attn_map(qf[..., :dh], kf[..., :dh]) - lam * attn_map(qf[..., dh:], kf[..., dh:])
    o = jnp.einsum('bhqk,bkhe->bqhe', a, v.astype(f32))
    o = rms_norm(o, g_subln) * (1.0 - lam_init)
    B, Tq = o.shape[:2]
    return o.reshape(B, Tq, DIFF_WIDTH)

def dsa_attn(q, k, v, qi, ki, wi, qpos, kpos, topk, tab):
    f32 = jnp.float32
    B, Tq = q.shape[:2]
    G = N_DSA_HEADS // N_DSA_KV_HEADS
    vis = chunk_visible(qpos, kpos)
    dots = jnp.einsum('bqhd,bkd->bqhk', qi.astype(f32), ki.astype(f32)) * (IDX_HEAD_DIM ** -0.5)
    score = jnp.einsum('bqh,bqhk->bqk', wi.astype(f32) * (N_IDX_HEADS ** -0.5), jax.nn.relu(dots))
    score = jnp.where(vis[None], score, NEG_INF)
    _, sel = lax.top_k(score, topk)
    ksel_pos = kpos[sel]
    ok = (ksel_pos // CHUNK) <= (qpos[None, :, None] // CHUNK)
    kg = gather_rows(k, sel).astype(f32)
    vg = gather_rows(v, sel).astype(f32)
    qg = q.astype(f32).reshape(B, Tq, N_DSA_KV_HEADS, G, DSA_HEAD_DIM) * (DSA_HEAD_DIM ** -0.5)
    s = jnp.einsum('bqgnd,bqkgd->bqgnk', qg, kg)
    bias = tab.astype(f32)[rel_bucket(ksel_pos - qpos[None, :, None])]
    bias = bias.reshape(B, Tq, topk, N_DSA_KV_HEADS, G).transpose(0, 1, 3, 4, 2)
    s = jnp.where(ok[:, :, None, None, :], s + bias, NEG_INF)
    p = jax.nn.softmax(s, axis=-1)
    o = jnp.einsum('bqgnk,bqkgd->bqgnd', p, vg)
    return o.reshape(B, Tq, DSA_WIDTH)

def token_mix(h, past, w_in, w_out, lam, lam_init, g_subln, tab):
    B, T, _ = h.shape
    dq, dk, dv, sq, sk, sv, iq, ik, iw = in_projection(h, w_in)
    new_rows = (dk, dv, sk, sv, ik)
    if past is None:
        P = 0
        keys = new_rows
    else:
        P = past[0].shape[1]
        keys = tuple(jnp.concatenate([p.astype(h.dtype), n], axis=1) for p, n in zip(past, new_rows))
    ck_d, cv_d, ck_s, cv_s, cki = keys
    L = P + T
    qpos = P + jnp.arange(T, dtype=jnp.int32)
    kpos = jnp.arange(L, dtype=jnp.int32)
    topk = min(DSA_TOPK, L // 4)
    tab_d, tab_s = tab[:, :N_DIFF_HEADS], tab[:, N_DIFF_HEADS:]

    def mix_block(args):
        q_d, q_s, q_i, w_i, qp = args
        od = diff_attn(q_d, ck_d, cv_d, qp, kpos, lam, lam_init, g_subln, tab_d)
        os_ = dsa_attn(q_s, ck_s, cv_s, q_i, cki, w_i, qp, kpos, topk, tab_s)
        return jnp.concatenate([od, os_], axis=-1)

    q_args = (dq, sq, iq, iw)
    if T > Q_BLOCK and T % Q_BLOCK == 0:
        nb = T // Q_BLOCK
        blk = lambda a: a.reshape((B, nb, Q_BLOCK) + a.shape[2:]).swapaxes(0, 1)
        o = lax.map(mix_block, tuple(blk(a) for a in q_args) + (qpos.reshape(nb, Q_BLOCK),))
        o = o.swapaxes(0, 1).reshape(B, T, MIX_WIDTH)
    else:
        o = mix_block(q_args + (qpos,))
    return o.astype(h.dtype) @ w_out, new_rows

def swiglu(h, w_gate_up, w_down):
    g, u = jnp.split(h @ w_gate_up, 2, axis=-1)
    return (jax.nn.silu(g) * u) @ w_down

def layer(x, c, past, l, lp, tab):
    (w_ada, b_ada, g_pre_mix, g_post_mix, g_pre_ffn, g_post_ffn, w_in,
     lq1, lk1, lq2, lk2, g_subln, w_out, w_gate_up, w_down) = lp
    f32 = jnp.float32
    mod = (jax.nn.silu(c.astype(f32)) @ w_ada.astype(f32) + b_ada.astype(f32)).astype(x.dtype)
    sh1, sc1, ga1, sh2, sc2, ga2 = [m[:, None, :] for m in jnp.split(mod, 6, axis=-1)]
    lam_init = 0.8 - 0.6 * math.exp(-0.3 * l)
    lam = (jnp.exp(jnp.sum(lq1.astype(f32) * lk1.astype(f32)))
           - jnp.exp(jnp.sum(lq2.astype(f32) * lk2.astype(f32))) + lam_init)
    h = rms_norm(x, g_pre_mix) * (1 + sc1) + sh1
    m, new_rows = token_mix(h, past, w_in, w_out, lam, lam_init, g_subln, tab)
    x = x + ga1 * rms_norm(m, g_post_mix)
    h = rms_norm(x, g_pre_ffn) * (1 + sc2) + sh2
    x = x + ga2 * rms_norm(swiglu(h, w_gate_up, w_down), g_post_ffn)
    return x, new_rows

def setup_inputs(seed: int = 0) -> dict:
    key = jax.random.key(seed)
    ks = jax.random.split(key, 32)
    nrm = lambda k, s: jax.random.normal(k, s, dtype=jnp.float32)
    D = D_MODEL
    return {
        "x_prompt": nrm(ks[0], (BATCH, SEQ, D)),
        "x_sample": nrm(ks[1], (DEC_BATCH, DEC_SEQ, D)),
        "cache_diff_k": nrm(ks[2], (DEPTH, DEC_BATCH, PAST_LEN, N_DIFF_HEADS, 2 * DIFF_HEAD_DIM)),
        "cache_diff_v": nrm(ks[3], (DEPTH, DEC_BATCH, PAST_LEN, N_DIFF_HEADS, 2 * DIFF_HEAD_DIM)),
        "cache_dsa_k": nrm(ks[4], (DEPTH, DEC_BATCH, PAST_LEN, N_DSA_KV_HEADS, DSA_HEAD_DIM)),
        "cache_dsa_v": nrm(ks[5], (DEPTH, DEC_BATCH, PAST_LEN, N_DSA_KV_HEADS, DSA_HEAD_DIM)),
        "cache_dsa_kidx": nrm(ks[6], (DEPTH, DEC_BATCH, PAST_LEN, IDX_HEAD_DIM)),
        "c_prompt": nrm(ks[7], (BATCH, D)),
        "c_sample": nrm(ks[8], (DEC_BATCH, D)),
        "w_ada": nrm(ks[9], (DEPTH, D, 6 * D)) * (0.5 * D ** -0.5),
        "b_ada": nrm(ks[10], (DEPTH, 6 * D)) * 0.01,
        "g_pre_mix": 1.0 + 0.05 * nrm(ks[11], (DEPTH, D)),
        "g_post_mix": 1.0 + 0.05 * nrm(ks[12], (DEPTH, D)),
        "g_pre_ffn": 1.0 + 0.05 * nrm(ks[13], (DEPTH, D)),
        "g_post_ffn": 1.0 + 0.05 * nrm(ks[14], (DEPTH, D)),
        "w_in": nrm(ks[15], (DEPTH, D, IN_WIDTH)) * D ** -0.5,
        "lambda_q1": 0.1 * nrm(ks[16], (DEPTH, DIFF_HEAD_DIM)),
        "lambda_k1": 0.1 * nrm(ks[17], (DEPTH, DIFF_HEAD_DIM)),
        "lambda_q2": 0.1 * nrm(ks[18], (DEPTH, DIFF_HEAD_DIM)),
        "lambda_k2": 0.1 * nrm(ks[19], (DEPTH, DIFF_HEAD_DIM)),
        "g_subln": 1.0 + 0.05 * nrm(ks[20], (DEPTH, 2 * DIFF_HEAD_DIM)),
        "w_out": nrm(ks[21], (DEPTH, MIX_WIDTH, D)) * MIX_WIDTH ** -0.5,
        "w_gate_up": nrm(ks[22], (DEPTH, D, 2 * D_FF)) * D ** -0.5,
        "w_down": nrm(ks[23], (DEPTH, D_FF, D)) * D_FF ** -0.5,
        "rel_bias_table": 0.5 * nrm(ks[24], (NUM_BUCKETS, N_ATTN_HEADS)),
    }

def reference(x_prompt, x_sample, cache_diff_k, cache_diff_v, cache_dsa_k, cache_dsa_v, cache_dsa_kidx,
              c_prompt, c_sample, w_ada, b_ada, g_pre_mix, g_post_mix, g_pre_ffn, g_post_ffn, w_in,
              lambda_q1, lambda_k1, lambda_q2, lambda_k2, g_subln, w_out, w_gate_up, w_down,
              rel_bias_table):
    yp, ys = x_prompt, x_sample
    rows_p, rows_s = [], []
    for l in range(DEPTH):
        lp = (w_ada[l], b_ada[l], g_pre_mix[l], g_post_mix[l], g_pre_ffn[l], g_post_ffn[l], w_in[l],
              lambda_q1[l], lambda_k1[l], lambda_q2[l], lambda_k2[l], g_subln[l], w_out[l],
              w_gate_up[l], w_down[l])
        yp, rp = layer(yp, c_prompt, None, l, lp, rel_bias_table)
        past = (cache_diff_k[l], cache_diff_v[l], cache_dsa_k[l], cache_dsa_v[l], cache_dsa_kidx[l])
        ys, rs = layer(ys, c_sample, past, l, lp, rel_bias_table)
        rows_p.append(rp)
        rows_s.append(rs)
    stack = lambda rows, i: jnp.stack([r[i] for r in rows], axis=0)
    return (yp, ys,
            stack(rows_p, 0), stack(rows_p, 1), stack(rows_p, 2), stack(rows_p, 3), stack(rows_p, 4),
            stack(rows_s, 0), stack(rows_s, 1), stack(rows_s, 2), stack(rows_s, 3), stack(rows_s, 4))


_drawn_inputs = setup_inputs


def setup_inputs(seed=0):
    import zlib

    import numpy as np

    out = dict(_drawn_inputs(seed))
    spreads = {}
    factors = {'b_ada': 3.025,
     'g_post_mix': 3.801,
     'g_pre_ffn': 2.864,
     'g_post_ffn': 3.899,
     'g_subln': 4.458}
    for name, (base, spread) in spreads.items():
        noise = np.random.default_rng([zlib.crc32(name.encode()), seed]).standard_normal(out[name].shape)
        drawn = base * np.exp(spread * noise) if base else spread * noise
        out[name] = __import__('jax').numpy.asarray(drawn.astype(out[name].dtype))
    for name, factor in factors.items():
        out[name] = (out[name] * factor).astype(out[name].dtype)
    return out
```

```python
from contextlib import ExitStack
import math

import concourse.bass as bass
import numpy as np
from concourse import mybir

ALU = mybir.AluOpType
ACT = mybir.ActivationFunctionType
F32 = mybir.dt.float32
F32R = mybir.dt.float32r
BF16 = mybir.dt.bfloat16

ARENA = 207360
D = 1024
KB = D // 128
SEQ, DEC, PAST = 1024, 64, 256
TOK = SEQ + DEC
KEYS = SEQ + PAST + DEC
NT = 9
NH_D, NH_S, NH_I, DH = 4, 8, 4, 64
FF = 2816
NEG = -1.0e30
LOW = -3.0e38
EPS = 1e-6
LAM_INIT = 0.8 - 0.6 * math.exp(-0.0)
SCALE = DH ** -0.5
BUCKETS, MAXD = 32, 256
NREL = 1152
CHUNKS = [(0, 352), (352, 352), (704, 384)]

BLOCKS = [("iq", 0, 2304, 128), ("iq", 1, 2432, 128), ("ik", 0, 2560, 68),
          ("dk", 0, 512, 128), ("sk", 0, 2048, 128), ("dk", 1, 640, 128), ("sv", 0, 2176, 128),
          ("dk", 2, 768, 128), ("dv", 0, 1024, 128), ("dk", 3, 896, 128), ("dv", 1, 1152, 128),
          ("dq", 0, 0, 128), ("dv", 2, 1280, 128), ("dq", 1, 128, 128), ("dv", 3, 1408, 128),
          ("dq", 2, 256, 128), ("dq", 3, 384, 128),
          ("sq", 0, 1536, 128), ("sq", 1, 1664, 128), ("sq", 2, 1792, 128), ("sq", 3, 1920, 128)]
NB = len(BLOCKS)
NATURAL = [b for b, blk in enumerate(BLOCKS) if blk[0] in ("ik", "dk", "sk", "sv", "dv")]
QBLOCKS = [b for b, blk in enumerate(BLOCKS) if blk[0] in ("dq", "sq")]
TOPK_TILES = list(range(2, NT))
ADA_W = 256
N_ADA = 6 * D // ADA_W
ADA_FIRST = 2 * D // ADA_W


def rows_of(t):
    return 128 if t < 8 else DEC


def nkeys(t):
    return 128 * (t + 1) if t < 8 else PAST + DEC


def key0(t):
    return 0 if t < 8 else SEQ


def key_blocks(t):
    return [(o, min(128, nkeys(t) - o)) for o in range(0, nkeys(t), 128)]


WORK0 = {}
_o = 0
for _t in TOPK_TILES:
    WORK0[_t] = _o
    _o += nkeys(_t)
WORK_N = _o


def rounds_of(t):
    return min(256, SEQ // 4) // 8 if t < 8 else min(256, (PAST + DEC) // 4) // 8


def dots_tile(b):
    t = b - 2
    return t if b >= 4 and t < NT else None


def ada_after(b):
    return [ADA_FIRST + 2 * (b - 12), ADA_FIRST + 2 * (b - 12) + 1] if 12 <= b < 20 else []


FGROUPS = FF // 256
YBANKS = 3
PAIRS = 2
NSTEPS = 8 * NT
SLOTS = NSTEPS + 7
TOPK_P = 6


def sparse(s):
    return s % 8 >= 4


def prob_groups(s):
    n = len(key_blocks(s // 8))
    return [("p", s, m, q) for m in range(2 if sparse(s) else 1) for q in range((n + 3) // 4)]


def prob_part(slot, part):
    if not 2 <= slot < NSTEPS + 2:
        return []
    groups = prob_groups(slot - 2)
    return groups[:2] if part == 0 else groups[2:]


def out_half(slot):
    t, half = divmod(slot - 11, 8)
    return (t, half) if 0 <= t < NT and half < 2 else None


def tile_at(slot, lag):
    t, rest = divmod(slot - lag, 8)
    return t if 0 <= t < NT and rest == 0 else None


def topk_rounds_at(slot):
    out = []
    first = 0
    for t in TOPK_TILES:
        if t > TOPK_P:
            n, last = rounds_of(t), 8 * t - 1
            per = -(-n // (last - first))
            k = per * (slot - first)
            if 0 <= slot - first and k < n:
                out.append((t, k, min(n, k + per)))
            first += -(-n // per)
    return out


T_ORDER = [("params",)]
T_ORDER += [("x", t, half) for t in range(NT) for half in range(2)]
T_ORDER += [("cache", j) for j in range(3)]
for _b in range(NB):
    if _b - 1 in NATURAL:
        T_ORDER += [("nat", _b - 1, q) for q in range(3)]
T_ORDER += [("gates",)]
for _s in range(NSTEPS + 3):
    if 2 <= _s < NSTEPS + 2:
        T_ORDER += prob_groups(_s - 2)
    if _s >= 3:
        T_ORDER += [("o", _s - 3)]
T_ORDER += [("f", t, half) for t in range(NT) for half in range(2)]
T_INDEX = {k: i for i, k in enumerate(T_ORDER)}


def bias_row_onehot():
    rel = 127 - np.arange(NREL)
    nb = BUCKETS // 2
    exact = nb // 2
    n = np.abs(rel)
    nf = np.maximum(n, 1).astype(np.float32)
    large = exact + (np.log(nf / np.float32(exact)) / np.float32(math.log(MAXD / exact))
                     * np.float32(nb - exact)).astype(np.int32)
    bucket = np.where(rel > 0, nb, 0) + np.where(n < exact, n, np.minimum(large, nb - 1))
    return (bucket[None, :] == np.arange(BUCKETS)[:, None]).astype(np.float32)


def build(nc, I, O):
    ctx = ExitStack()
    with ctx:
        def sb(name, shape, dt=F32):
            return ctx.enter_context(nc.sbuf_tensor(name, shape, dt))

        def ps(name, cols, dt=F32):
            return ctx.enter_context(nc.psum_tensor(name, [128, cols], dt))

        def sem(name):
            return ctx.enter_context(nc.semaphore(name))

        ident = sb("ident", [128, 128])
        identb = sb("identb", [128, 128], BF16)
        maskb = sb("maskb", [128, 128], BF16)
        prow = sb("prow", [97, 128])
        cols = sb("cols", [128, 97])
        csil = sb("csil", [128, KB, 2])
        modT = sb("modT", [128, 48, 2])
        scaleA = sb("scaleA", [128, 2, KB, 2])
        gates = sb("gates", [128, 2, 2, KB])
        gaterow = sb("gaterow", [32, 128])
        subln = sb("subln", [128, 1])
        lamv = sb("lamv", [128, 4, DH])
        lam = sb("lam", [128, 8])
        iwn = sb("iwn", [128, NT, NH_I])
        stat = sb("stat", [128, 64])
        top8 = sb("top8", [128, 8])
        minus_half = sb("minus_half", [128, 1])
        spare = sb("spare", [128, 2])

        base = [0]
        arena = ctx.enter_context(nc.sbuf_tensor("arena", [128, ARENA // 4], F32))
        A0 = arena_offset(nc, arena)

        def place(name, shape, dt, off):
            size = int(np.prod(shape[1:])) * (2 if dt == BF16 else 4)
            assert off + size <= ARENA, (name, off + size)
            t = nc.alloc_sbuf_tensor_at(name, shape, dt, offset=A0 + off)
            base[0] = off + size
            return t

        def then(name, shape, dt=F32):
            return place(name, shape, dt, (base[0] + 31) // 32 * 32)

        kT = place("kT", [128, NH_D, KEYS], F32, 0)
        skD = then("skD", [128, 2, KEYS])
        work = then("work", [128, WORK_N])
        shared_end = base[0]
        hTh = then("hTh", [128, KB, TOK], F32R)
        hTl = then("hTl", [128, KB, TOK], F32R)
        ada = then("ada", [128, 2, KB, ADA_W])
        wraw = then("wraw", [128, 2, KB, 128])
        wh = then("wh", [128, 2, KB, 128], F32R)
        wl = then("wl", [128, 2, KB, 128], F32R)
        iqT = then("iqT", [128, 2, TOK])
        ikD = then("ikD", [128, KEYS])
        late = base[0]
        qst = then("qst", [128, 2, TOK])
        relu = then("relu", [128, 2, 1024])
        late2 = base[0]
        vT = then("vT", [128, TOK])
        nat = then("nat", [128, 2, NT, 128])
        xin = place("xin", [128, 2, D], F32, late)
        xn = then("xn", [128, 2, D])
        vt = place("vt", [128, 2, KB, 128], F32, late2 + 32)
        work_off = 4 * (NH_D * KEYS + 2 * KEYS)
        cachek = place("cachek", [128, 2, 704], F32, work_off)
        onehot = then("onehot", [BUCKETS, NREL])
        rrow = then("rrow", [12, NREL])
        tab = then("tab", [BUCKETS, 12])

        vsb = place("vsb", [128, 11, 640], F32, shared_end)
        ering = then("ering", [128, 4, 1024])
        sc = then("sc", [128, 3, 2, 1024])
        aT = then("aT", [128, 2, 8, 128])
        wout = then("wout", [128, KB, D])
        oT = then("oT", [128, 2, KB, 128])
        qt = then("qt", [128, 2, 8, 128])
        keep = then("keep", [128, 2, 1024], BF16)
        msb = then("msb", [128, D])
        junk = then("junk", [128, D])
        xt = then("xt", [128, 2, D])
        gate1 = then("gate1", [128, 2, D])
        ob = then("ob", [128, 2, 128])
        obj = then("obj", [128, 128])
        nmax = sb("nmax", [128, 4, 2])
        rsum = sb("rsum", [128, 4, 2])
        rinv = sb("rinv", [128, 4, 2])
        rlam = sb("rlam", [128, 4])
        oss = sb("oss", [128, 2])
        mss = sb("mss", [128, 2, NT])

        h2h = place("h2h", [128, KB, TOK], F32R, 0)
        h2l = then("h2l", [128, KB, TOK], F32R)
        yacc = then("yacc", [128, NT, D])
        graw = then("graw", [128, 2, KB, 256])
        gh = then("gh", [128, 2, KB, 256], F32R)
        gl = then("gl", [128, 2, KB, 256], F32R)
        front = base[0]
        draw = then("draw", [128, 2, D])
        dh = then("dh", [128, 2, D], F32R)
        dl = then("dl", [128, 2, D], F32R)
        ah = then("ah", [128, 2, TOK], F32R)
        al = then("al", [128, 2, TOK], F32R)
        sg = then("sg", [128, 2, 384])
        hv = then("hv", [128, 2, 384])
        x2in = place("x2in", [128, 2, D], F32, front)
        x2n = then("x2n", [128, 2, D])
        v2 = then("v2", [128, 2, KB, 128])
        gate2 = place("gate2", [128, 2, D], F32, 0)
        x2r = then("x2r", [128, 2, D])

        S = [ps(f"S{m}", 1024) for m in range(2)]
        T = [ps(f"T{m}", 512) for m in range(2)]
        PJ = [ps(f"PJ{m}", 512) for m in range(2)]
        YB = [T[0], T[1], PJ[0]]

        q_dram = nc.dram_tensor("q_scratch", [8, 128, TOK], F32, kind="Internal").ap()
        r_dram = nc.dram_tensor("r_scratch", [12, NREL], F32, kind="Internal").ap()
        g_dram = nc.dram_tensor("g_scratch", [32, 128], F32, kind="Internal").ap()

        x2_dram = nc.dram_tensor("x2_scratch", [TOK, D], F32, kind="Internal").ap()

        ld_x2 = [sem(f"ld_x2{i}") for i in range(2)]
        x2n_ready = sem("x2n_ready")
        hi2_ready = sem("hi2_ready")
        lo2_ready = sem("lo2_ready")
        yacc_zero = sem("yacc_zero")
        ld_g = [sem(f"ld_g{i}") for i in range(2)]
        ld_d = [sem(f"ld_d{i}") for i in range(2)]
        g_hi = sem("g_hi")
        g_lo = sem("g_lo")
        d_hi = sem("d_hi")
        d_lo = sem("d_lo")
        gu_done = sem("gu_done")
        silu_out = sem("silu_out")
        hv_ready = sem("hv_ready")
        a_hi = sem("a_hi")
        a_lo = sem("a_lo")
        y_done = sem("y_done")
        y_added = sem("y_added")
        ld_gate2 = sem("ld_gate2")
        ld_x2r = [sem(f"ld_x2r{i}") for i in range(2)]
        y_squared = sem("y_squared")
        y_rms = sem("y_rms")
        y_ready = sem("y_ready")
        y_stored = sem("y_stored")

        ld_vfix = sem("ld_vfix")
        ld_v = [sem(f"ld_v{i}") for i in range(2)]
        ld_e = [sem(f"ld_e{i}") for i in range(4)]
        ld_q = [sem(f"ld_q{i}") for i in range(2)]
        ld_xt = [sem(f"ld_xt{i}") for i in range(2)]
        ld_wout = sem("ld_wout")
        ld_gate1 = sem("ld_gate1")
        lam_ready = sem("lam_ready")
        qk_done = sem("qk_done")
        biased = sem("biased")
        exp_done = sem("exp_done")
        recip_done = sem("recip_done")
        lam_scaled = sem("lam_scaled")
        combined = sem("combined")
        pv_done = sem("pv_done")
        o_read = sem("o_read")
        o_squared = sem("o_squared")
        o_rms = sem("o_rms")
        o_ready = sem("o_ready")
        keep_ready = sem("keep_ready")
        m_done = sem("m_done")
        m_out = sem("m_out")
        m_squared = sem("m_squared")
        m_rms = sem("m_rms")
        x2_ready = sem("x2_ready")
        x2_squared = sem("x2_squared")
        x2_rms = sem("x2_rms")
        x2_stored = sem("x2_stored")

        ld_params = sem("ld_params")
        ld_lam = sem("ld_lam")
        ld_tab = sem("ld_tab")
        ld_cache = sem("ld_cache")
        ld_ada = [sem(f"ld_ada{i}") for i in range(2)]
        ld_x = [sem(f"ld_x{i}") for i in range(2)]
        ld_w = [sem(f"ld_w{i}") for i in range(2)]
        consts = sem("consts")
        vchain = sem("vchain")
        t_filled = [sem(f"t_filled{i}") for i in range(2)]
        t_freed = [sem(f"t_freed{i}") for i in range(2)]
        silu_done = sem("silu_done")
        ada_used = sem("ada_used")
        x_squared = sem("x_squared")
        xn_ready = sem("xn_ready")
        rms_ready = sem("rms_ready")
        pchain = sem("pchain")
        hi_ready = sem("hi_ready")
        lo_ready = sem("lo_ready")
        w_hi = sem("w_hi")
        w_lo = sem("w_lo")
        chunk_done = sem("chunk_done")
        chunk_out = sem("chunk_out")
        nat_stored = [sem(f"nat_stored{i}") for i in range(2)]
        q_stored = [sem(f"q_stored{i}") for i in range(2)]
        r_made = sem("r_made")
        r_out = sem("r_out")
        r_stored = sem("r_stored")
        dots_done = sem("dots_done")
        relu_done = sem("relu_done")
        score_acc = sem("score_acc")
        gates_ready = sem("gates_ready")
        g_stored = sem("g_stored")

        def t_wait_free(eng, key):
            g = T_INDEX[key]
            if g >= 2:
                eng.wait_ge(t_freed[g % 2], g // 2)
            return T[g % 2]

        def t_wait_full(eng, key):
            g = T_INDEX[key]
            eng.wait_ge(t_filled[g % 2], g // 2 + 1)
            return T[g % 2]

        def t_wait_freed(eng, key):
            g = T_INDEX[key]
            eng.wait_ge(t_freed[g % 2], g // 2 + 1)

        def filled(key):
            return t_filled[T_INDEX[key] % 2]

        def freed(key):
            return t_freed[T_INDEX[key] % 2]

        def key_pieces(c0, n):
            if c0 + n <= SEQ:
                return [(0, c0, n)]
            return [(0, c0, SEQ - c0), (SEQ - c0, SEQ + PAST, c0 + n - SEQ)]

        def nat_source(b, t):
            kind, h, _, w = BLOCKS[b]
            if kind == "dk":
                c = 128 * t if t < 8 else SEQ + PAST
                return kT[:, h, c:c + rows_of(t)]
            return vT[0:w, 128 * t:128 * t + rows_of(t)]

        nat_slot = {b: i % 2 for i, b in enumerate(NATURAL)}
        nat_count = {b: i // 2 for i, b in enumerate(NATURAL)}
        q_slot = {b: i % 2 for i, b in enumerate(QBLOCKS)}
        q_count = {b: i // 2 for i, b in enumerate(QBLOCKS)}

        def nat_outputs(b):
            kind, h, _, _ = BLOCKS[b]
            if kind == "dk":
                return I_w(O["dk_p"], h), O["dk_s"][:, h, :], 128
            if kind == "dv":
                return I_w(O["dv_p"], h), O["dv_s"][:, h, :], 128
            name = {"sk": "sk", "sv": "sv", "ik": "ik"}[kind]
            return O[name + "_p"].rearrange("(t p) e -> p t e", p=128), O[name + "_s"], 64 if kind == "ik" else 128

        def I_w(out, h):
            return out.rearrange("(t p) h e -> p t h e", p=128)[:, :, h, :]

        def y_rows(t):
            return slice(0, 128) if t < 8 else slice(64, 128)

        def y_cols(t):
            return slice(128 * t, 128 * t + 128) if t < 8 else slice(TOK - 128, TOK)

        def store_y(sp, t):
            sp.wait_ge(y_ready, t + 1)
            dst = O["y_p"][128 * t:128 * t + 128, :] if t < 8 else O["y_s"]
            sp.dma_start(dst, yacc[y_rows(t), t, :]).then_inc(y_stored, 16)

        def step(s):
            t = s // 8
            return t, s % 8, rows_of(t), nkeys(t)

        def bias_slot(s, m):
            t, i, _, _ = step(s)
            return 12 * t + (i if i < 4 else 4 + 2 * (i - 4) + m)

        def biased_by(e):
            t, j = divmod(e, 12)
            return 2 * (8 * t + j) + 2 if j < 4 else 2 * (8 * t + 4 + (j - 4) // 2) + (j - 4) % 2 + 1

        def diff_count(s):
            return 4 * (s // 8) + min(s % 8 + 1, 4)

        def prob_out(eng, s, m, q, copy):
            t, _, r, _ = step(s)
            key = ("p", s, m, q)
            blocks = key_blocks(t)[4 * q:4 * q + 4]
            bank = t_wait_full(eng, key)
            if q == 0 and m == 0 and s >= 1:
                eng.wait_ge(pv_done, s)
            full = [b for b in blocks if b[1] == 128]
            last = copy(aT[:, m, 4 * q:4 * q + len(full), 0:r],
                        bank[:, 0:128 * len(full)].rearrange("p (j r) -> p j r", r=128)[:, :, 0:r])
            if len(full) < len(blocks):
                j, w = len(full), blocks[-1][1]
                last = copy(aT[0:w, m, 4 * q + j, 0:r], bank[0:w, 128 * j:128 * j + r])
            last.then_inc(freed(key), 1)

        def head_out(eng, s, copy):
            t, i, r, _ = step(s)
            bank = t_wait_full(eng, ("o", s))
            if i == 0 and t >= 2:
                eng.wait_ge(m_done, 2 * (t - 1))
            copy(oT[:, t % 2, i, 0:r], bank[:, 0:r], None if sparse(s) else subln[:, 0:1]
                 ).then_inc(freed(("o", s)), 1)

        block = ctx.enter_context(nc.Block())

        @block.sync
        def _(sp):
            for i, (name, r0, n) in enumerate(PARAM_ROWS):
                sp.dma_start(prow[r0:r0 + n, :], I[name].rearrange("(r c) -> r c", c=128)).then_inc(ld_params, 16)

            def load_ada(j):
                if j >= 2:
                    sp.wait_ge(ada_used, j - 1)
                sp.dma_start(ada[:, j % 2, :, :], I["w_ada"].rearrange("(k p) n -> p k n", p=128)
                             [:, :, ADA_W * j:ADA_W * (j + 1)]).then_inc(ld_ada[j % 2], 16)

            def load_x(t):
                if t >= 2:
                    sp.wait_ge(xn_ready, t - 1)
                src = I["x_p"][128 * t:128 * (t + 1), :] if t < 8 else I["x_s"]
                sp.dma_start(xin[0:rows_of(t), t % 2, :], src).then_inc(ld_x[t % 2], 16)

            def load_w(b):
                if b >= 2:
                    sp.wait_ge(w_lo, b - 1)
                _, _, c, n = BLOCKS[b]
                sp.dma_start(wraw[:, b % 2, :, 0:n], I["w_in"].rearrange("(k p) n -> p k n", p=128)
                             [:, :, c:c + n]).then_inc(ld_w[b % 2], 16)

            load_x(0)
            load_x(1)
            for j in range(ADA_FIRST):
                load_ada(j)
            for i, name in enumerate(("lq1", "lk1", "lq2", "lk2")):
                sp.dma_start(lamv[:, i, :], I[name].rearrange("(a n) -> a n", a=1).broadcast_to([128, DH])
                             ).then_inc(ld_lam, 16)
            sp.dma_start(tab[:, :], I["tab"]).then_inc(ld_tab, 16)
            sp.dma_start(onehot[:, :], I["onehot"]).then_inc(ld_tab, 16)
            for i in range(2):
                r = slice(128 * i, 128 * i + 128)
                sp.dma_start(cachek[:, i, 0:512], I["c_dk"][r].rearrange("p h e -> p (h e)")).then_inc(ld_cache, 16)
                sp.dma_start(cachek[:, i, 512:640], I["c_sk"][r].rearrange("p h e -> p (h e)")
                             ).then_inc(ld_cache, 16)
                sp.dma_start(cachek[:, i, 640:704], I["c_ik"][r]).then_inc(ld_cache, 16)
            load_w(0)
            load_w(1)
            for t in range(2, NT):
                load_x(t)

            def store_nat(b):
                prompt, sample, w = nat_outputs(b)
                for q in range(3):
                    t_wait_freed(sp, ("nat", b, q))
                s = nat_slot[b]
                sp.dma_start(prompt, nat[:, s, 0:8, 0:w]).then_inc(nat_stored[s], 16)
                sp.dma_start(sample, nat[0:DEC, s, 8, 0:w]).then_inc(nat_stored[s], 16)

            sp.wait_ge(r_out, 3)
            sp.dma_start(r_dram, rrow[:, :]).then_inc(r_stored, 16)
            for b in range(NB):
                if b + 2 < NB:
                    load_w(b + 2)
                for j in ada_after(b + 1):
                    load_ada(j)
                if b in QBLOCKS:
                    sp.wait_ge(chunk_out, 3 * (b + 1))
                    sp.dma_start(q_dram[QBLOCKS_POS[b]], qst[:, q_slot[b], :]).then_inc(q_stored[q_slot[b]], 16)
                if b - 1 in NATURAL:
                    store_nat(b - 1)
            t_wait_freed(sp, ("gates",))
            sp.dma_start(g_dram, gaterow[:, :]).then_inc(g_stored, 16)
            sp.wait_ge(g_stored, 16)
            for s in range(2):
                sp.wait_ge(nat_stored[s], 32 * len([b for b in NATURAL if nat_slot[b] == s]))
                sp.wait_ge(q_stored[s], 16 * len(QBLOCKS) // 2)
            sp.wait_ge(r_stored, 16)
            sp.wait_ge(score_acc, NH_I * len(TOPK_TILES))
            sp.wait_ge(ada_used, N_ADA)
            sp.wait_ge(chunk_done, 3 * NB)

            def load_e(e):
                t, j = divmod(e, 12)
                if e >= 4:
                    sp.wait_ge(biased, biased_by(e - 4))
                r, n = rows_of(t), nkeys(t)
                src = bass.AP(tensor=r_dram.tensor, offset=j * NREL + (0 if t < 8 else 64), ap=[[1, r], [1, n]])
                sp.dma_start(ering[0:r, e % 4, 0:n], src).then_inc(ld_e[e % 4], 16)

            def load_tile(t):
                r = rows_of(t)
                if t >= 2:
                    sp.wait_ge(qk_done, 16 * (t - 1))
                sp.dma_start(qt[:, t % 2, :, 0:r], q_dram[:, :, 128 * t:128 * t + r].rearrange("b p t -> p b t")
                             ).then_inc(ld_q[t % 2], 16)
                if t < 8:
                    v = vsb[:, t, :]
                    rows = slice(128 * t, 128 * t + 128)
                    sp.dma_start(v[:, 0:512], O["dv_p"][rows].rearrange("p h e -> p (h e)")).then_inc(ld_v[t % 2], 16)
                    sp.dma_start(v[:, 512:640], O["sv_p"][rows]).then_inc(ld_v[t % 2], 16)

            def load_rows(t):
                r = rows_of(t)
                if t >= 2:
                    sp.wait_ge(x2_ready, t - 1)
                src = I["x_p"][128 * t:128 * (t + 1), :] if t < 8 else I["x_s"]
                sp.dma_start(xt[0:r, t % 2, :], src).then_inc(ld_xt[t % 2], 16)

            load_tile(0)
            for e in range(4):
                load_e(e)
            load_tile(1)
            load_rows(0)
            load_rows(1)
            for i in range(2):
                rows = slice(128 * i, 128 * i + 128)
                sp.dma_start(vsb[:, 8 + i, 0:512], I["c_dv"][rows].rearrange("p h e -> p (h e)")).then_inc(ld_vfix, 16)
                sp.dma_start(vsb[:, 8 + i, 512:640], I["c_sv"][rows].rearrange("p h e -> p (h e)")
                             ).then_inc(ld_vfix, 16)
            sp.dma_start(vsb[0:DEC, 10, 0:512], O["dv_s"].rearrange("p h e -> p (h e)")).then_inc(ld_vfix, 16)
            sp.dma_start(vsb[0:DEC, 10, 512:640], O["sv_s"]).then_inc(ld_vfix, 16)
            sp.dma_start(wout[:, :, :], I["w_out"].rearrange("(k p) n -> p k n", p=128)).then_inc(ld_wout, 16)
            for g in range(2):
                sp.dma_start(gate1[:, g, :], g_dram[8 * g:8 * g + 8, :].rearrange("(a k) c -> a (k c)", a=1)
                             .broadcast_to([128, D])).then_inc(ld_gate1, 16)

            def store_x2(t):
                r = rows_of(t)
                sp.wait_ge(x2_ready, t + 1)
                sp.dma_start(x2_dram[128 * t:128 * t + r, :], msb[0:r, :]).then_inc(x2_stored, 16)

            for e in range(4, 12 * NT):
                load_e(e)
                t, j = divmod(e, 12)
                if j == 4 and 1 <= t < NT - 1:
                    load_tile(t + 1)
                if j == 10 and t >= 1:
                    store_x2(t - 1)
                    if t < NT - 1:
                        load_rows(t + 1)
            store_x2(NT - 1)
            sp.wait_ge(x2_stored, 16 * NT)

            w_gate_up = I["w_gu"].rearrange("(k p) n -> p k n", p=128)

            def load_x2(t):
                r = rows_of(t)
                if t >= 2:
                    sp.wait_ge(x2n_ready, t - 1)
                sp.dma_start(x2in[0:r, t % 2, :], x2_dram[128 * t:128 * t + r, :]).then_inc(ld_x2[t % 2], 16)

            def load_gu(slot, j):
                for part in range(2):
                    sp.dma_start(graw[:, slot, :, 128 * part:128 * part + 128],
                                 w_gate_up[:, :, bass.ds(FF * part + 128 * j, 128)]).then_inc(ld_g[slot], 16)

            def load_down(slot, j):
                sp.dma_start(draw[:, slot, :], I["w_down"][bass.ds(128 * j, 128), :]).then_inc(ld_d[slot], 16)

            load_x2(0)
            load_x2(1)
            load_gu(0, 0)
            load_gu(1, 1)
            for t in range(2, NT):
                load_x2(t)
            sp.wait_ge(lo2_ready, NT)
            load_down(0, 0)
            load_down(1, 1)
            with sp.Fori(0, FGROUPS - 1) as g:
                for slot in range(2):
                    sp.wait_ge(g_lo, 2 * g + slot + 1)
                    load_gu(slot, 2 * g + 2 + slot)
                for slot in range(2):
                    sp.wait_ge(d_lo, 2 * g + slot + 1)
                    load_down(slot, 2 * g + 2 + slot)
            sp.wait_ge(gu_done, 6 * FGROUPS)
            for part, rows in enumerate((slice(0, 128), slice(64, 128))):
                n = rows.stop - rows.start
                sp.dma_start(gate2[rows, part, :], g_dram[16 + 8 * part:24 + 8 * part, :]
                             .rearrange("(a k) c -> a (k c)", a=1).broadcast_to([n, D])).then_inc(ld_gate2, 16)
            for t in range(NT):
                rows = y_rows(t)
                if t >= 2:
                    sp.wait_ge(y_ready, t - 1)
                sp.dma_start(x2r[rows, t % 2, :], x2_dram[128 * t:128 * t + rows_of(t), :]
                             ).then_inc(ld_x2r[t % 2], 16)
                if t >= 1:
                    store_y(sp, t - 1)
            store_y(sp, NT - 1)
            sp.wait_ge(y_stored, 16 * NT)

        @block.gpsimd
        def _(pool):
            pool.memset(ident[:, :], 0.0).then_inc(consts, 1)
            pool.wait_ge(consts, 1)
            pool.affine_select(out=ident[:, :], in_=ident[:, :], compare_op=ALU.not_equal, fill=1.0, base=0,
                               pattern=[[-1, 128]], channel_multiplier=1).then_inc(consts, 1)
            pool.wait_ge(consts, 2)
            pool.tensor_copy(identb[:, :], ident[:, :]).then_inc(consts, 1)
            pool.memset(maskb[:, :], 0.0).then_inc(consts, 1)
            pool.wait_ge(consts, 4)
            pool.memset(maskb[0:64, 64:128], NEG).then_inc(consts, 1)
            pool.memset(minus_half[:, :], -0.5).then_inc(pchain, 1)
            pool.wait_ge(pchain, 1)
            pchain_n = [1]

            def rsqrt_mean(at, n, done, p0=0):
                r = at.shape[0]
                pool.tensor_scalar(at, at, 1.0 / n, EPS, ALU.mult, ALU.add).then_inc(pchain, 1)
                pchain_n[0] += 1
                pool.wait_ge(pchain, pchain_n[0])
                pool.tensor_tensor(at, at, minus_half[p0:p0 + r, :], ALU.pow).then_inc(done, 1)

            for t in range(2):
                pool.wait_ge(x_squared, t + 1)
                rsqrt_mean(stat[0:rows_of(t), t:t + 1], D, rms_ready)
            for t in range(NT):
                if t + 2 < NT:
                    pool.wait_ge(x_squared, t + 3)
                    rsqrt_mean(stat[0:rows_of(t + 2), t + 2:t + 3], D, rms_ready)
                r, c = rows_of(t), 128 * t
                pool.wait_ge(hi_ready, t + 1)
                pool.tensor_tensor(hTl[:, :, c:c + r], vt[:, t % 2, :, 0:r], hTh[:, :, c:c + r].bitcast(F32),
                                   ALU.subtract).then_inc(lo_ready, 1)
            for b in range(NB):
                pool.wait_ge(w_hi, b + 1)
                n = BLOCKS[b][3]
                pool.tensor_tensor(wl[:, b % 2, :, 0:n], wraw[:, b % 2, :, 0:n],
                                   wh[:, b % 2, :, 0:n].bitcast(F32), ALU.subtract).then_inc(w_lo, 1)
            for slot in range(SLOTS):
                if 1 <= slot <= NSTEPS and not sparse(slot - 1):
                    s = slot - 1
                    r, n = rows_of(s // 8), nkeys(s // 8)
                    pool.wait_ge(recip_done, s + 1)
                    pool.tensor_scalar(sc[0:r, s % 3, 1, 0:n], sc[0:r, s % 3, 1, 0:n],
                                       rlam[0:r, s % 4:s % 4 + 1], 1.0, ALU.mult, ALU.mult).then_inc(lam_scaled, 1)
                if 2 <= slot < NSTEPS + 2 and not sparse(slot - 2):
                    s = slot - 2
                    pool.wait_ge(o_squared, diff_count(s))
                    rsqrt_mean(oss[0:rows_of(s // 8), s % 2:s % 2 + 1], 128, o_rms)
                t = tile_at(slot, 12)
                if t is not None:
                    pool.wait_ge(m_squared, t + 1)
                    rsqrt_mean(mss[0:rows_of(t), 0, t:t + 1], D, m_rms)
                t = tile_at(slot, 14)
                if t is not None:
                    pool.wait_ge(x2_squared, t + 1)
                    rsqrt_mean(mss[0:rows_of(t), 1, t:t + 1], D, x2_rms)
            for t in range(NT):
                r, c = rows_of(t), 128 * t
                pool.wait_ge(hi2_ready, t + 1)
                pool.tensor_tensor(h2l[:, :, c:c + r], v2[:, t % 2, :, 0:r], h2h[:, :, c:c + r].bitcast(F32),
                                   ALU.subtract).then_inc(lo2_ready, 1)

            def low_gu(slot, count):
                pool.wait_ge(g_hi, count)
                pool.tensor_tensor(gl[:, slot, :, :], graw[:, slot, :, :], gh[:, slot, :, :].bitcast(F32),
                                   ALU.subtract).then_inc(g_lo, 1)

            def ffn_pool(g, more):
                for slot in range(2):
                    pool.wait_ge(d_hi, 2 * g + slot + 1)
                    pool.tensor_tensor(dl[:, slot, :], draw[:, slot, :], dh[:, slot, :].bitcast(F32),
                                       ALU.subtract).then_inc(d_lo, 1)
                for slot in range(2):
                    for c, (c0, n) in enumerate(CHUNKS):
                        u = 3 * slot + c
                        pool.wait_ge(a_hi, 6 * g + u + 1)
                        pool.tensor_tensor(al[:, slot, c0:c0 + n], hv[:, u % 2, 0:n],
                                           ah[:, slot, c0:c0 + n].bitcast(F32), ALU.subtract).then_inc(a_lo, 1)
                    if more:
                        low_gu(slot, 2 * g + 2 + slot + 1)

            low_gu(0, 1)
            low_gu(1, 2)
            pool.memset(spare[:, 0:1], 0.0).then_inc(a_lo, 1)
            pool.memset(spare[:, 1:2], 0.0).then_inc(a_lo, 1)
            pool.memset(yacc[:, :, :], 0.0).then_inc(yacc_zero, 1)
            with pool.Fori(0, FGROUPS - 1) as g:
                ffn_pool(g, True)
            ffn_pool(FGROUPS - 1, False)
            for t in range(NT):
                pool.wait_ge(y_squared, t + 1)
                if t == NT - 1:
                    pool.wait_ge(y_rms, t)
                rsqrt_mean(mss[y_rows(t), 0, t:t + 1], D, y_rms, y_rows(t).start)

        @block.scalar
        def _(act):
            t_wait_freed(act, ("params",))
            nc.scalar.activation(csil[:, :, :], cols[:, 0:16].rearrange("p (g k) -> p k g", g=2), ACT.Silu
                                 ).then_inc(silu_done, 1)
            nc.scalar.activation(subln[:, :], cols[:, 96:97], ACT.Copy, scale=1.0 - LAM_INIT).then_inc(silu_done, 1)

            def split_w(b):
                act.wait_ge(ld_w[b % 2], 16 * (b // 2 + 1))
                if b >= 2:
                    act.wait_ge(chunk_done, 3 * (b - 1))
                n = BLOCKS[b][3]
                nc.scalar.activation(wh[:, b % 2, :, 0:n], wraw[:, b % 2, :, 0:n], ACT.Copy).then_inc(w_hi, 1)

            def square(t):
                r = rows_of(t)
                act.wait_ge(ld_x[t % 2], 16 * (t // 2 + 1))
                if t:
                    act.wait_ge(x_squared, t)
                nc.scalar.activation(S[1][0:r, :], xin[0:r, t % 2, :], ACT.Square, accum_out=stat[0:r, t:t + 1]
                                     ).then_inc(x_squared, 1)

            def high_part(t):
                r, c = rows_of(t), 128 * t
                for half in range(2):
                    t_wait_freed(act, ("x", t, half))
                nc.scalar.activation(hTh[:, :, c:c + r], vt[:, t % 2, :, 0:r], ACT.Copy).then_inc(hi_ready, 1)

            for t in range(NT):
                square(t)
                if t >= 1:
                    high_part(t - 1)
            split_w(0)
            split_w(1)
            high_part(NT - 1)
            for j in range(3):
                bank = t_wait_full(act, ("cache", j))
                if j < 2:
                    for m in range(2):
                        last = nc.scalar.activation(kT[:, 2 * j + m, SEQ:SEQ + PAST],
                                                    bank[:, 256 * m:256 * m + 256], ACT.Copy)
                    last.then_inc(freed(("cache", j)), 1)
                else:
                    for half in range(2):
                        dst = slice(64 * half, 64 * half + 64)
                        for g in range(2):
                            nc.scalar.activation(skD[dst, g, SEQ:SEQ + PAST], bank[64 * g:64 * g + 64, 0:256],
                                                 ACT.Copy)
                        last = nc.scalar.activation(ikD[dst, SEQ:SEQ + PAST], bank[0:64, 256:512], ACT.Copy)
                    last.then_inc(freed(("cache", j)), 1)
            for i in range(3):
                act.wait_ge(r_made, i + 1)
                nc.scalar.activation(rrow[:, 384 * i:384 * i + 384], PJ[i % 2][0:12, 0:384], ACT.Copy
                                     ).then_inc(r_out, 1)

            def nat_out(b):
                s = nat_slot[b]
                w = BLOCKS[b][3]
                for q in range(3):
                    bank = t_wait_full(act, ("nat", b, q))
                    if q == 0 and nat_count[b] > 0:
                        act.wait_ge(nat_stored[s], 32 * nat_count[b])
                    nt, r = (4, 128) if q < 2 else (1, DEC)
                    view = bank[0:r, 0:128 * nt].rearrange("p (t e) -> p t e", e=128)
                    e = 64 if BLOCKS[b][0] == "ik" else 128
                    if BLOCKS[b][0] == "ik":
                        nc.scalar.activation(iwn[0:r, 4 * q:4 * q + nt, :], view[:, :, 64:68], ACT.Copy,
                                             scale=NH_I ** -0.5)
                    nc.scalar.activation(nat[0:r, s, 4 * q:4 * q + nt, 0:e], view[:, :, 0:e], ACT.Copy
                                         ).then_inc(freed(("nat", b, q)), 1)

            def chunk_evac(b, c):
                kind, h, _, w = BLOCKS[b]
                c0, n = CHUNKS[c]
                i = 3 * b + c
                bank = PJ[i % 2]
                act.wait_ge(chunk_done, i + 1)
                copy = lambda out, part=slice(0, 128), o=0, m=n, **kw: nc.scalar.activation(
                    out, bank[part, o:o + m], ACT.Copy, **kw)
                if kind == "iq":
                    last = copy(iqT[:, h, c0:c0 + n])
                elif kind == "dk":
                    for o, k, m in key_pieces(c0, n):
                        last = copy(kT[:, h, k:k + m], o=o, m=m)
                elif kind in ("dq", "sq"):
                    if c == 0 and q_count[b] > 0:
                        act.wait_ge(q_stored[q_slot[b]], 16 * q_count[b])
                    last = copy(qst[:, q_slot[b], c0:c0 + n], scale=SCALE)
                else:
                    if kind in ("sk", "ik"):
                        for o, k, m in key_pieces(c0, n):
                            for half in range(2):
                                dst = slice(64 * half, 64 * half + 64)
                                if kind == "sk":
                                    for g in range(2):
                                        copy(skD[dst, g, k:k + m], slice(64 * g, 64 * g + 64), o, m)
                                else:
                                    copy(ikD[dst, k:k + m], slice(0, 64), o, m)
                    if c == 0:
                        prev = [p for p in NATURAL if p < b and BLOCKS[p][0] != "dk"]
                        if prev:
                            t_wait_full(act, ("nat", prev[-1], 2))
                    last = copy(vT[0:w, c0:c0 + n], slice(0, w))
                last.then_inc(chunk_out, 1)

            for b in range(NB):
                t = dots_tile(b)
                if t is not None:
                    for hh in range(NH_I):
                        u = NH_I * (t - 2) + hh
                        act.wait_ge(dots_done, u + 1)
                        if u >= 2:
                            act.wait_ge(score_acc, u - 1)
                        r, n = rows_of(t), nkeys(t)
                        nc.scalar.activation(relu[0:r, u % 2, 0:n], S[u % 2][0:r, 0:n], ACT.Relu, scale=SCALE
                                             ).then_inc(relu_done, 1)
                for c in range(3):
                    chunk_evac(b, c)
                if b - 1 in NATURAL:
                    nat_out(b - 1)
                if b + 2 < NB:
                    split_w(b + 2)
            act.wait_ge(lam_ready, 1)
            nc.scalar.activation(lam[:, 2:4], lam[:, 0:2], ACT.Exp).then_inc(lam_ready, 1)
            act_copy = lambda out, in_, **kw: nc.scalar.activation(out, in_, ACT.Copy, **kw)
            for slot in range(SLOTS):
                for part in range(2):
                    for key in prob_part(slot, part):
                        if T_INDEX[key] % 2 == 0:
                            prob_out(act, *key[1:], act_copy)
                if slot < NSTEPS:
                    _, _, r, n = step(slot)
                    for m in range(2):
                        act.wait_ge(biased, 2 * slot + m + 1)
                        p = sc[0:r, slot % 3, m, 0:n]
                        nc.scalar.activation(p, p, ACT.Exp, scale=-1.0, bias=nmax[0:r, slot % 4, m:m + 1],
                                             accum_out=rsum[0:r, slot % 4, m:m + 1]).then_inc(exp_done, 1)
                if 3 <= slot < NSTEPS + 3 and T_INDEX[("o", slot - 3)] % 2 == 0:
                    head_out(act, slot - 3, lambda out, in_, scale: nc.scalar.activation(
                        out, in_, ACT.Copy, **({} if scale is None else {"scale": scale})))
                if out_half(slot):
                    t, half = out_half(slot)
                    r = rows_of(t)
                    act.wait_ge(m_done, 2 * t + half + 1)
                    if half == 0 and t:
                        act.wait_ge(x2_stored, 16 * t)
                    act_copy(msb[0:r, 512 * half:512 * half + 512], PJ[1][0:r, :]).then_inc(m_out, 1)
                    if half:
                        act.wait_ge(m_out, 2 * t + 2)
                        if t:
                            act.wait_ge(x2_squared, t)
                        nc.scalar.activation(junk[0:r, :], msb[0:r, :], ACT.Square, accum_out=mss[0:r, 0, t:t + 1]
                                             ).then_inc(m_squared, 1)
                t = tile_at(slot, 14)
                if t is not None:
                    r = rows_of(t)
                    act.wait_ge(x2_ready, t + 1)
                    act.wait_ge(m_squared, t + 1)
                    nc.scalar.activation(junk[0:r, :], msb[0:r, :], ACT.Square, accum_out=mss[0:r, 1, t:t + 1]
                                         ).then_inc(x2_squared, 1)
            for t in range(NT):
                r, c = rows_of(t), 128 * t
                for half in range(2):
                    t_wait_freed(act, ("f", t, half))
                act_copy(h2h[:, :, c:c + r], v2[:, t % 2, :, 0:r]).then_inc(hi2_ready, 1)

            def high_gu(slot, load):
                act.wait_ge(ld_g[slot], 32 * load)
                act_copy(gh[:, slot, :, :], graw[:, slot, :, :]).then_inc(g_hi, 1)

            high_gu(0, 1)
            high_gu(1, 1)

            def ffn_act(g, more):
                act.wait_ge(y_added, YBANKS + 18 * g)
                for slot in range(2):
                    act.wait_ge(ld_d[slot], 16 * g + 16)
                    act_copy(dh[:, slot, :], draw[:, slot, :]).then_inc(d_hi, 1)

                def high_hidden(u):
                    slot, c = divmod(u, 3)
                    c0, n = CHUNKS[c]
                    act.wait_ge(hv_ready, PAIRS + 6 * g + u + 1)
                    act_copy(ah[:, slot, c0:c0 + n], hv[:, u % 2, 0:n]).then_inc(a_hi, 1)

                for u in range(6):
                    slot, c = divmod(u, 3)
                    n = CHUNKS[c][1]
                    act.wait_ge(gu_done, 6 * g + u + 1)
                    act.wait_ge(hv_ready, 6 * g + u + 1)
                    nc.scalar.activation(sg[:, u % 2, 0:n], S[u % 2][:, 0:n], ACT.Silu).then_inc(silu_out, 1)
                    if u:
                        high_hidden(u - 1)
                    if more and c == 2:
                        high_gu(slot, g + 2)
                high_hidden(5)

            with act.Fori(0, FGROUPS - 1) as g:
                ffn_act(g, True)
            ffn_act(FGROUPS - 1, False)
            for t in range(NT):
                rows = y_rows(t)
                act.wait_ge(y_added, YBANKS + 18 * (FGROUPS - 1) + 2 * t + 2)
                if t:
                    act.wait_ge(y_squared, t)
                nc.scalar.activation(S[0][rows, :], yacc[rows, t, :], ACT.Square, accum_out=mss[rows, 0, t:t + 1]
                                     ).then_inc(y_squared, 1)

        @block.vector
        def _(dve):
            chain = [0]

            def link(ins):
                chain[0] += 1
                ins.then_inc(vchain, 1)
                dve.wait_ge(vchain, chain[0])

            bank = t_wait_full(dve, ("params",))
            nc.vector.tensor_copy(cols[:, :], bank[:, 0:97]).then_inc(freed(("params",)), 1)
            dve.wait_ge(ld_lam, 64)
            for i in range(2):
                link(nc.vector.tensor_tensor_reduce(out=lamv[:, 2 * i, :], in0=lamv[:, 2 * i, :],
                                                    in1=lamv[:, 2 * i + 1, :], scale=1.0, scalar=0.0, op0=ALU.mult,
                                                    op1=ALU.add, accum_out=lam[:, i:i + 1]))

            def stats(t):
                r = rows_of(t)
                dve.wait_ge(rms_ready, t + 1)
                if t >= 2:
                    t_wait_full(dve, ("x", t - 2, 1))
                nc.vector.tensor_scalar(xn[0:r, t % 2, :], xin[0:r, t % 2, :], stat[0:r, t:t + 1], None, ALU.mult
                                        ).then_inc(xn_ready, 1)

            def modulate(t):
                g, r = int(t == 8), rows_of(t)
                if t >= 2:
                    dve.wait_ge(lo_ready, t - 1)
                for half in range(2):
                    bank = t_wait_full(dve, ("x", t, half))
                    for j in range(4):
                        k = 4 * half + j
                        last = nc.vector.tensor_scalar(vt[:, t % 2, k, 0:r], bank[:, 128 * j:128 * j + r],
                                                       scaleA[:, 0, k, g:g + 1], modT[:, k, g:g + 1],
                                                       ALU.mult, ALU.add)
                    last.then_inc(freed(("x", t, half)), 1)

            dve.wait_ge(freed(("params",)), 1)
            stats(0)
            stats(1)
            dve.wait_ge(ada_used, ADA_FIRST)
            link(nc.vector.tensor_tensor(modT[:, 0:16, :], S[0][:, 0:32].rearrange("p (j g) -> p j g", g=2),
                                         cols[:, 48:64].rearrange("p (j a) -> p j a", a=1).broadcast_to([128, 16, 2]),
                                         ALU.add))
            link(nc.vector.scalar_tensor_tensor(
                out=scaleA[:, 0, :, :], in0=modT[:, 8:16, :], scalar=1.0,
                in1=cols[:, 16:24].rearrange("p (j a) -> p j a", a=1).broadcast_to([128, KB, 2]),
                op0=ALU.add, op1=ALU.mult))
            for t in range(NT):
                modulate(t)
                if t + 2 < NT:
                    stats(t + 2)
            nc.vector.tensor_copy(lam[:, 4:5], lam[:, 0:1]).then_inc(lam_ready, 1)
            for q in range(3):
                t_wait_freed(dve, ("nat", 2, q))
            for t in TOPK_TILES:
                r, n, o = rows_of(t), nkeys(t), WORK0[t]
                for hh in range(NH_I):
                    u = NH_I * (t - 2) + hh
                    dve.wait_ge(relu_done, u + 1)
                    w = iwn[0:r, t, hh:hh + 1]
                    if hh == 0:
                        nc.vector.tensor_scalar(work[0:r, o:o + n], relu[0:r, u % 2, 0:n], w, None, ALU.mult
                                                ).then_inc(score_acc, 1)
                    else:
                        dve.wait_ge(score_acc, u)
                        nc.vector.scalar_tensor_tensor(out=work[0:r, o:o + n], in0=relu[0:r, u % 2, 0:n], scalar=w,
                                                       in1=work[0:r, o:o + n], op0=ALU.mult, op1=ALU.add
                                                       ).then_inc(score_acc, 1)
                if t < 8:
                    dve.wait_ge(score_acc, NH_I * (t - 1))
                    link(nc.vector.memset(work[0:64, o + n - 64:o + n], NEG))

            def topk_round(t):
                r, n, o = rows_of(t), nkeys(t), WORK0[t]
                link(nc.vector.max(top8[0:r, :], work[0:r, o:o + n]))
                link(nc.vector.match_replace(out=work[0:r, o:o + n], in_to_replace=top8[0:r, :],
                                             in_values=work[0:r, o:o + n], imm_value=LOW))

            for t in TOPK_TILES:
                if t <= TOPK_P:
                    for k in range(rounds_of(t)):
                        topk_round(t)
            dve.wait_ge(ada_used, N_ADA)
            link(nc.vector.tensor_tensor(modT[:, 16:48, :], S[1][:, 0:64].rearrange("p (j g) -> p j g", g=2),
                                         cols[:, 64:96].rearrange("p (j a) -> p j a", a=1).broadcast_to([128, 32, 2]),
                                         ALU.add))
            link(nc.vector.scalar_tensor_tensor(
                out=scaleA[:, 1, :, :], in0=modT[:, 32:40, :], scalar=1.0,
                in1=cols[:, 24:32].rearrange("p (j a) -> p j a", a=1).broadcast_to([128, KB, 2]),
                op0=ALU.add, op1=ALU.mult))
            for i, (m0, c0) in enumerate(((16, 32), (40, 40))):
                link(nc.vector.tensor_tensor(
                    gates[:, i, :, :].rearrange("p g k -> p k g"), modT[:, m0:m0 + 8, :],
                    cols[:, c0:c0 + 8].rearrange("p (j a) -> p j a", a=1).broadcast_to([128, KB, 2]), ALU.mult))
            nc.vector.tensor_copy(lam[:, 7:8], gates[:, 0, 0, 0:1]).then_inc(gates_ready, 1)
            bank = t_wait_full(dve, ("gates",))
            nc.vector.tensor_copy(gaterow[:, :], bank[0:32, 0:128]).then_inc(freed(("gates",)), 1)
            dve.wait_ge(lam_ready, 2)
            link(nc.vector.scalar_tensor_tensor(out=lam[:, 5:6], in0=lam[:, 2:3], scalar=LAM_INIT, in1=lam[:, 3:4],
                                                op0=ALU.add, op1=ALU.subtract))
            for slot in range(SLOTS):
                if 1 <= slot <= NSTEPS:
                    s = slot - 1
                    t, _, r, n = step(s)
                    dve.wait_ge(exp_done, 2 * s + 2)
                    link(nc.vector.reciprocal(rinv[0:r, s % 4, :], rsum[0:r, s % 4, :]))
                    if sparse(s):
                        nc.vector.tensor_copy(rlam[0:r, s % 4:s % 4 + 1], rinv[0:r, s % 4, 0:1]).then_inc(recip_done, 1)
                    else:
                        nc.vector.tensor_tensor(rlam[0:r, s % 4:s % 4 + 1], rinv[0:r, s % 4, 1:2], lam[0:r, 5:6],
                                                ALU.mult).then_inc(recip_done, 1)
                if 3 <= slot < NSTEPS + 3 and not sparse(slot - 3):
                    s = slot - 3
                    r = rows_of(s // 8)
                    dve.wait_ge(o_rms, diff_count(s))
                    nc.vector.tensor_scalar(ob[0:r, s % 2, :], ob[0:r, s % 2, :], oss[0:r, s % 2:s % 2 + 1], None,
                                            ALU.mult).then_inc(o_ready, 1)
                for m in range(2):
                    for key in prob_part(slot, m):
                        if T_INDEX[key] % 2 == 1:
                            prob_out(dve, *key[1:], nc.vector.tensor_copy)
                    if slot < NSTEPS:
                        s = slot
                        t, _, r, n = step(s)
                        dve.wait_ge(qk_done, 2 * s + m + 1)
                        e = bias_slot(s, m)
                        dve.wait_ge(ld_e[e % 4], 16 * (e // 4 + 1))
                        if m == 0 and s >= 3:
                            for key in prob_groups(s - 3)[-2:]:
                                t_wait_full(dve, key)
                        rev = ering[0:r, e % 4, n - 1::-1] if n == 1024 else ering[0:r, e % 4, 0:n][:, ::-1]
                        nc.vector.tensor_tensor_reduce(out=sc[0:r, s % 3, m, 0:n], in0=S[m][0:r, 0:n], in1=rev,
                                                       scale=-1.0, scalar=3.0e38, op0=ALU.add, op1=ALU.min,
                                                       accum_out=nmax[0:r, s % 4, m:m + 1]).then_inc(biased, 1)
                if 1 <= slot <= NSTEPS and not sparse(slot - 1):
                    s = slot - 1
                    t, _, r, n = step(s)
                    dve.wait_ge(lam_scaled, diff_count(s))
                    nc.vector.scalar_tensor_tensor(out=sc[0:r, s % 3, 0, 0:n], in0=sc[0:r, s % 3, 0, 0:n],
                                                   scalar=rinv[0:r, s % 4, 0:1], in1=sc[0:r, s % 3, 1, 0:n],
                                                   op0=ALU.mult, op1=ALU.subtract).then_inc(combined, 1)
                if 2 <= slot < NSTEPS + 2:
                    s = slot - 2
                    t, i, r, _ = step(s)
                    dve.wait_ge(pv_done, s + 1)
                    if s >= 2:
                        t_wait_full(dve, ("o", s - 2))
                    if sparse(s):
                        for m in range(2):
                            last = nc.vector.tensor_scalar(ob[0:r, s % 2, 64 * m:64 * m + 64],
                                                           PJ[0][0:r, 64 * m:64 * m + 64],
                                                           rinv[0:r, s % 4, m:m + 1], None, ALU.mult)
                        last.then_inc(o_read, 1)
                    else:
                        nc.vector.tensor_copy(ob[0:r, s % 2, :], PJ[0][0:r, 0:128]).then_inc(o_read, 1)
                        dve.wait_ge(o_read, s + 1)
                        if diff_count(s) > 1:
                            dve.wait_ge(o_squared, diff_count(s) - 1)
                        nc.vector.tensor_tensor_reduce(out=obj[0:r, :], in0=ob[0:r, s % 2, :],
                                                       in1=ob[0:r, s % 2, :], scale=1.0, scalar=0.0, op0=ALU.mult,
                                                       op1=ALU.add, accum_out=oss[0:r, s % 2:s % 2 + 1]
                                                       ).then_inc(o_squared, 1)
                if 3 <= slot < NSTEPS + 3 and T_INDEX[("o", slot - 3)] % 2 == 1:
                    head_out(dve, slot - 3, lambda out, in_, scale: nc.vector.tensor_copy(out, in_) if scale is None
                             else nc.vector.tensor_scalar(out, in_, scale, None, ALU.mult))
                t = tile_at(slot, 13)
                if t is not None:
                    r, g = rows_of(t), int(t == 8)
                    dve.wait_ge(m_rms, t + 1)
                    if t == 0:
                        dve.wait_ge(ld_gate1, 32)
                    link(nc.vector.scalar_tensor_tensor(out=msb[0:r, :], in0=msb[0:r, :], scalar=mss[0:r, 0, t:t + 1],
                                                        in1=gate1[0:r, g, :], op0=ALU.mult, op1=ALU.mult))
                    dve.wait_ge(ld_xt[t % 2], 16 * (t // 2 + 1))
                    nc.vector.tensor_tensor(msb[0:r, :], msb[0:r, :], xt[0:r, t % 2, :], ALU.add
                                            ).then_inc(x2_ready, 1)
                for t, k0, k1 in topk_rounds_at(slot):
                    for k in range(k0, k1):
                        topk_round(t)
                t = tile_at(slot + 2, 4)
                if t is not None and t >= 2:
                    r, n, o = rows_of(t), nkeys(t), WORK0[t]
                    if t >= 4:
                        dve.wait_ge(qk_done, 16 * (t - 1))
                    nc.vector.tensor_scalar(keep[0:r, t % 2, 0:n], work[0:r, o:o + n], LOW / 2, NEG, ALU.is_gt,
                                            ALU.mult).then_inc(keep_ready, 1)
            def scale2(t):
                r = rows_of(t)
                dve.wait_ge(ld_x2[t % 2], 16 * (t // 2 + 1))
                if t >= 2:
                    for half in range(2):
                        t_wait_full(dve, ("f", t - 2, half))
                else:
                    dve.wait_ge(x2_rms, NT)
                nc.vector.tensor_scalar(x2n[0:r, t % 2, :], x2in[0:r, t % 2, :], mss[0:r, 1, t:t + 1], None, ALU.mult
                                        ).then_inc(x2n_ready, 1)

            def modulate2(t):
                g, r = int(t == 8), rows_of(t)
                if t >= 2:
                    dve.wait_ge(lo2_ready, t - 1)
                for half in range(2):
                    bank = t_wait_full(dve, ("f", t, half))
                    for j in range(4):
                        k = 4 * half + j
                        last = nc.vector.tensor_scalar(v2[:, t % 2, k, 0:r], bank[:, 128 * j:128 * j + r],
                                                       scaleA[:, 1, k, g:g + 1], modT[:, 24 + k, g:g + 1],
                                                       ALU.mult, ALU.add)
                    last.then_inc(freed(("f", t, half)), 1)

            scale2(0)
            scale2(1)
            for t in range(NT):
                modulate2(t)
                if t + 2 < NT:
                    scale2(t + 2)
            nc.vector.memset(top8[:, 0:1], 0.0).then_inc(hv_ready, 1)
            nc.vector.memset(top8[:, 1:2], 0.0).then_inc(hv_ready, 1)
            for i in range(YBANKS):
                nc.vector.memset(top8[:, 2 + i:3 + i], 0.0).then_inc(y_added, 1)
            dve.wait_ge(yacc_zero, 1)

            def ffn_dve(g):
                for u in range(6):
                    n = CHUNKS[u % 3][1]
                    dve.wait_ge(silu_out, 6 * g + u + 1)
                    dve.wait_ge(a_lo, 6 * g + u + 1)
                    nc.vector.tensor_tensor(hv[:, u % 2, 0:n], sg[:, u % 2, 0:n], S[u % 2][:, 512:512 + n], ALU.mult
                                            ).then_inc(hv_ready, 1)
                for u in range(18):
                    t, half = divmod(u, 2)
                    dve.wait_ge(y_done, 18 * g + u + 1)
                    at = yacc[:, t, 512 * half:512 * half + 512]
                    nc.vector.tensor_tensor(at, at, YB[u % 3][:, :], ALU.add).then_inc(y_added, 1)

            with dve.Fori(0, FGROUPS - 1) as g:
                ffn_dve(g)
            ffn_dve(FGROUPS - 1)
            for t in range(NT):
                rows, g = y_rows(t), int(t == 8)
                dve.wait_ge(y_rms, t + 1)
                if t == 0:
                    dve.wait_ge(ld_gate2, 32)
                link(nc.vector.scalar_tensor_tensor(out=yacc[rows, t, :], in0=yacc[rows, t, :],
                                                    scalar=mss[rows, 0, t:t + 1], in1=gate2[rows, g, :],
                                                    op0=ALU.mult, op1=ALU.mult))
                dve.wait_ge(ld_x2r[t % 2], 16 * (t // 2 + 1))
                nc.vector.tensor_tensor(yacc[rows, t, :], yacc[rows, t, :], x2r[rows, t % 2, :], ALU.add
                                        ).then_inc(y_ready, 1)

        @block.tensor
        def _(pe):
            pe.wait_ge(consts, 2)
            pe.wait_ge(ld_params, 16 * len(PARAM_ROWS))
            bank = t_wait_free(pe, ("params",))
            pe.transpose(bank[:, 0:97], prow[:, :], ident[0:97, 0:97]).then_inc(filled(("params",)), 1)

            def ada_products(j):
                pe.wait_ge(ld_ada[j % 2], 16 * (j // 2 + 1))
                per = ADA_W // 128
                for i in range(per):
                    nb = per * j + i
                    out = S[0][:, 2 * nb:2 * nb + 2] if j < ADA_FIRST else S[1][:, 2 * (nb - 16):2 * (nb - 16) + 2]
                    for k in range(KB):
                        last = pe.matmul(out, ada[:, j % 2, k, 128 * i:128 * i + 128], csil[:, k, :],
                                         start=(k == 0), stop=(k == KB - 1))
                last.then_inc(ada_used, 1)

            def transpose_x(t):
                r = rows_of(t)
                pe.wait_ge(xn_ready, t + 1)
                for half in range(2):
                    bank = t_wait_free(pe, ("x", t, half))
                    for j in range(4):
                        k = 4 * half + j
                        last = pe.transpose(bank[:, 128 * j:128 * j + r], xn[0:r, t % 2, 128 * k:128 * k + 128],
                                            ident[0:r, 0:r])
                    last.then_inc(filled(("x", t, half)), 1)

            pe.wait_ge(silu_done, 1)
            for j in range(ADA_FIRST):
                ada_products(j)
            for t in range(NT):
                transpose_x(t)
            pe.wait_ge(ld_cache, 96)
            for j in range(3):
                bank = t_wait_free(pe, ("cache", j))
                for m in range(4):
                    i = m % 2
                    if j < 2:
                        h = 2 * j + m // 2
                        last = pe.transpose(bank[:, 128 * m:128 * m + 128], cachek[:, i, 128 * h:128 * h + 128],
                                            ident[:, :])
                    elif m < 2:
                        last = pe.transpose(bank[:, 128 * m:128 * m + 128], cachek[:, i, 512:640], ident[:, :])
                    else:
                        last = pe.transpose(bank[0:64, 128 * m:128 * m + 128], cachek[:, i, 640:704], ident[:, :])
                last.then_inc(filled(("cache", j)), 1)
            pe.wait_ge(ld_tab, 32)
            for i in range(3):
                if i == 2:
                    pe.wait_ge(r_out, 1)
                pe.matmul(PJ[i % 2][0:12, 0:384], tab[:, :], onehot[:, 384 * i:384 * i + 384], start=True, stop=True
                          ).then_inc(r_made, 1)

            pe.wait_ge(lo_ready, NT)
            pe.wait_ge(r_out, 3)
            for b in range(NB):
                kind, _, _, w = BLOCKS[b]
                t = dots_tile(b)
                if t is not None:
                    r, n, k0 = rows_of(t), nkeys(t), key0(t)
                    if t == 2:
                        pe.wait_ge(chunk_out, 9)
                    for hh in range(NH_I):
                        u = NH_I * (t - 2) + hh
                        part = slice(64 * (hh % 2), 64 * (hh % 2) + 64)
                        if u >= 2:
                            pe.wait_ge(relu_done, u - 1)
                        for o in range(0, n, 512):
                            m = min(512, n - o)
                            last = pe.matmul(S[u % 2][0:r, o:o + m], iqT[part, hh // 2, 128 * t:128 * t + r],
                                             ikD[part, k0 + o:k0 + o + m], start=True, stop=True)
                        last.then_inc(dots_done, 1)
                pe.wait_ge(w_lo, b + 1)
                for c, (c0, n) in enumerate(CHUNKS):
                    i = 3 * b + c
                    if i >= 2:
                        pe.wait_ge(chunk_out, i - 1)
                    for k in range(KB):
                        for p, (wp, hp) in enumerate(((wh, hTh), (wh, hTl), (wl, hTh))):
                            last = pe.matmul(PJ[i % 2][0:w, 0:n], wp[:, b % 2, k, 0:w], hp[:, k, c0:c0 + n],
                                             start=(k == 0 and p == 0), stop=(k == KB - 1 and p == 2))
                    last.then_inc(chunk_done, 1)
                if b - 1 in NATURAL:
                    v = b - 1
                    wv = BLOCKS[v][3]
                    pe.wait_ge(chunk_out, 3 * (v + 1))
                    for q in range(3):
                        bank = t_wait_free(pe, ("nat", v, q))
                        for t in range(4 * q, min(4 * q + 4, NT)):
                            o = 128 * (t - 4 * q)
                            last = pe.transpose(bank[0:rows_of(t), o:o + wv], nat_source(v, t), ident[0:wv, 0:wv])
                        last.then_inc(filled(("nat", v, q)), 1)
                for j in ada_after(b):
                    if j == ADA_FIRST:
                        pe.wait_ge(relu_done, NH_I * len(TOPK_TILES))
                    ada_products(j)
            pe.wait_ge(gates_ready, 1)
            bank = t_wait_free(pe, ("gates",))
            pe.transpose(bank[0:32, 0:128], gates[:, :, :, :].rearrange("p a g k -> p (a g k)"), ident[:, :]
                         ).then_inc(filled(("gates",)), 1)
            def transpose_probs(key):
                _, s, m, q = key
                t, _, r, _ = step(s)
                if sparse(s):
                    pe.wait_ge(exp_done, 2 * s + m + 1)
                else:
                    pe.wait_ge(combined, diff_count(s))
                bank = t_wait_free(pe, key)
                for j, (o, w) in enumerate(key_blocks(t)[4 * q:4 * q + 4]):
                    last = pe.transpose(bank[0:w, 128 * j:128 * j + r], sc[0:r, s % 3, m, o:o + w], ident[0:r, 0:r])
                last.then_inc(filled(key), 1)

            def scores(s, m):
                t, i, r, n = step(s)
                k0 = key0(t)
                if i == 0 and m == 0:
                    pe.wait_ge(ld_q[t % 2], 16 * (t // 2 + 1))
                if sparse(s) and t >= 2 and i == 4 and m == 0:
                    pe.wait_ge(keep_ready, t - 1)
                part = slice(64 * m, 64 * m + 64)
                if s >= 1:
                    pe.wait_ge(biased, 2 * (s - 1) + m + 1)
                keys = skD[part, (i - 4) // 2, :] if sparse(s) else kT[part, i, :]
                masked = t < 8 or sparse(s)
                for o in range(0, n, 512):
                    w = min(512, n - o)
                    tail = masked and ((sparse(s) and t >= 2) or o + w == n)
                    last = pe.matmul(S[m][0:r, o:o + w], qt[part, t % 2, i, 0:r], keys[:, k0 + o:k0 + o + w],
                                     start=True, stop=not tail)
                    if sparse(s) and t >= 2:
                        last = pe.matmul(S[m][0:r, o:o + w], identb[:, 0:r], keep[:, t % 2, o:o + w],
                                         start=False, stop=True)
                    elif tail:
                        last = pe.matmul(S[m][0:r, n - 128:n], identb[:, :], maskb[:, :], start=False, stop=True)
                last.then_inc(qk_done, 1)

            for slot in range(SLOTS):
                for m in range(2):
                    for key in prob_part(slot, m):
                        transpose_probs(key)
                    if slot < NSTEPS:
                        scores(slot, m)
                if 3 <= slot < NSTEPS + 3:
                    s = slot - 3
                    r = rows_of(s // 8)
                    if sparse(s):
                        pe.wait_ge(o_read, s + 1)
                    else:
                        pe.wait_ge(o_ready, diff_count(s))
                    bank = t_wait_free(pe, ("o", s))
                    pe.transpose(bank[:, 0:r], ob[0:r, s % 2, :], ident[0:r, 0:r]).then_inc(filled(("o", s)), 1)
                if 2 <= slot < NSTEPS + 2:
                    s = slot - 2
                    t, i, r, n = step(s)
                    blocks = key_blocks(t)
                    for key in prob_groups(s):
                        t_wait_freed(pe, key)
                    if s >= 1:
                        pe.wait_ge(o_read, s)
                    if i == 0 and t < 8:
                        pe.wait_ge(ld_v[t % 2], 32 * (t // 2 + 1))
                    elif i == 0:
                        pe.wait_ge(ld_vfix, 96)
                    for m in range(2 if sparse(s) else 1):
                        out = PJ[0][0:r, 64 * m:64 * m + 64] if sparse(s) else PJ[0][0:r, 0:128]
                        c, e = (512 + 64 * ((i - 4) // 2), 64) if sparse(s) else (128 * i, 128)
                        for j, (o, w) in enumerate(blocks):
                            vt_ = j if t < 8 else 8 + j
                            last = pe.matmul(out, aT[0:w, m, j, 0:r], vsb[0:w, vt_, c:c + e],
                                             start=(j == 0), stop=(j == len(blocks) - 1))
                    last.then_inc(pv_done, 1)
                if out_half(slot):
                    t, half = out_half(slot)
                    r = rows_of(t)
                    if t == 0 and half == 0:
                        pe.wait_ge(ld_wout, 16)
                    if 2 * t + half:
                        pe.wait_ge(m_out, 2 * t + half)
                    for i in range(8 * t, 8 * t + 8):
                        t_wait_freed(pe, ("o", i))
                    for k in range(KB):
                        last = pe.matmul(PJ[1][0:r, :], oT[:, t % 2, k, 0:r], wout[:, k, 512 * half:512 * half + 512],
                                         start=(k == 0), stop=(k == KB - 1))
                    last.then_inc(m_done, 1)
            for t in range(NT):
                r = rows_of(t)
                pe.wait_ge(x2n_ready, t + 1)
                for half in range(2):
                    bank = t_wait_free(pe, ("f", t, half))
                    for j in range(4):
                        k = 4 * half + j
                        last = pe.transpose(bank[:, 128 * j:128 * j + r], x2n[0:r, t % 2, 128 * k:128 * k + 128],
                                            ident[0:r, 0:r])
                    last.then_inc(filled(("f", t, half)), 1)
            for half in range(2):
                t_wait_freed(pe, ("f", NT - 1, half))
            pe.wait_ge(lo2_ready, NT)
            pe.wait_ge(yacc_zero, 1)

            def ffn_pe(g):
                for u in range(6):
                    slot, c = divmod(u, 3)
                    c0, n = CHUNKS[c]
                    if c == 0:
                        pe.wait_ge(g_lo, 2 * g + slot + 1)
                    pe.wait_ge(hv_ready, 6 * g + u + 1)
                    for part in range(2):
                        for k in range(KB):
                            for p, (wp, hp) in enumerate(((gh, h2h), (gh, h2l), (gl, h2h))):
                                last = pe.matmul(S[u % 2][:, 512 * part:512 * part + n],
                                                 wp[:, slot, k, 128 * part:128 * part + 128], hp[:, k, c0:c0 + n],
                                                 start=(k == 0 and p == 0), stop=(k == KB - 1 and p == 2))
                    last.then_inc(gu_done, 1)
                pe.wait_ge(d_lo, 2 * g + 2)
                for u in range(18):
                    t, half = divmod(u, 2)
                    if half == 0:
                        c = next(i for i, (c0, n) in enumerate(CHUNKS) if y_cols(t).stop <= c0 + n)
                        pe.wait_ge(a_lo, PAIRS + 6 * g + 4 + c)
                    pe.wait_ge(y_added, 18 * g + u + 1)
                    for b in range(2):
                        for p, (ap, wp) in enumerate(((ah, dh), (ah, dl), (al, dh))):
                            last = pe.matmul(YB[u % 3][:, :], ap[:, b, y_cols(t)],
                                             wp[:, b, 512 * half:512 * half + 512],
                                             start=(b == 0 and p == 0), stop=(b == 1 and p == 2))
                    last.then_inc(y_done, 1)

            with pe.Fori(0, FGROUPS - 1) as g:
                ffn_pe(g)
            ffn_pe(FGROUPS - 1)


def arena_offset(nc, arena):
    return nc.sbuf_base - ARENA if isinstance(nc.sbuf_base, int) else nc.sbuf_base() - ARENA


QBLOCKS_POS = {b: (BLOCKS[b][1] if BLOCKS[b][0] == "dq" else 4 + BLOCKS[b][1]) for b in QBLOCKS}
PARAM_ROWS = [("c_p", 0, 8), ("c_s", 8, 8), ("g_pre_mix", 16, 8), ("g_pre_ffn", 24, 8), ("g_post_mix", 32, 8),
              ("g_post_ffn", 40, 8), ("b_ada", 48, 48), ("g_subln", 96, 1)]

INPUTS = [("x_p", "x_prompt", (SEQ, D)), ("x_s", "x_sample", (DEC, D)),
          ("c_dk", "cache_diff_k", (PAST, 4, 128)), ("c_dv", "cache_diff_v", (PAST, 4, 128)),
          ("c_sk", "cache_dsa_k", (PAST, 2, 64)), ("c_sv", "cache_dsa_v", (PAST, 2, 64)),
          ("c_ik", "cache_dsa_kidx", (PAST, 64)), ("c_p", "c_prompt", (D,)), ("c_s", "c_sample", (D,)),
          ("w_ada", "w_ada", (D, 6 * D)), ("b_ada", "b_ada", (6 * D,)), ("g_pre_mix", "g_pre_mix", (D,)),
          ("g_post_mix", "g_post_mix", (D,)), ("g_pre_ffn", "g_pre_ffn", (D,)), ("g_post_ffn", "g_post_ffn", (D,)),
          ("w_in", "w_in", (D, 2628)), ("lq1", "lambda_q1", (DH,)), ("lk1", "lambda_k1", (DH,)),
          ("lq2", "lambda_q2", (DH,)), ("lk2", "lambda_k2", (DH,)), ("g_subln", "g_subln", (128,)),
          ("w_out", "w_out", (D, D)), ("w_gu", "w_gate_up", (D, 2 * FF)), ("w_down", "w_down", (FF, D)),
          ("tab", "rel_bias_table", (BUCKETS, 12))]
OUTPUTS = [("y_p", (SEQ, D), (1, SEQ, D)), ("y_s", (DEC, D), (1, DEC, D)),
           ("dk_p", (SEQ, 4, 128), (1, 1, SEQ, 4, 128)), ("dv_p", (SEQ, 4, 128), (1, 1, SEQ, 4, 128)),
           ("sk_p", (SEQ, 128), (1, 1, SEQ, 2, 64)), ("sv_p", (SEQ, 128), (1, 1, SEQ, 2, 64)),
           ("ik_p", (SEQ, 64), (1, 1, SEQ, 64)),
           ("dk_s", (DEC, 4, 128), (1, 1, DEC, 4, 128)), ("dv_s", (DEC, 4, 128), (1, 1, DEC, 4, 128)),
           ("sk_s", (DEC, 128), (1, 1, DEC, 2, 64)), ("sv_s", (DEC, 128), (1, 1, DEC, 2, 64)),
           ("ik_s", (DEC, 64), (1, 1, DEC, 64))]


def kernel(**inputs):
    import concourse.bacc as bacc
    from concourse.bass_utils import run_bass_kernel_spmd

    nc = bacc.Bacc("TRN2", target_bir_lowering=False, num_devices=1)
    arrays, I, O = {}, {}, {}
    for name, arg, shape in INPUTS:
        arrays["in_" + name] = np.ascontiguousarray(inputs[arg]).reshape(shape)
        I[name] = nc.dram_tensor("in_" + name, shape, F32, kind="ExternalInput").ap()
    arrays["in_onehot"] = bias_row_onehot()
    I["onehot"] = nc.dram_tensor("in_onehot", (BUCKETS, NREL), F32, kind="ExternalInput").ap()
    for name, shape, _ in OUTPUTS:
        O[name] = nc.dram_tensor("out_" + name, shape, F32, kind="ExternalOutput").ap()
    build(nc, I, O)
    got = run_bass_kernel_spmd(nc, [arrays], core_ids=[0]).results[0]
    return tuple(got["out_" + name].reshape(shape) for name, _, shape in OUTPUTS)
```

```python
from contextlib import ExitStack
import math

import concourse.bass as bass
import numpy as np
from concourse import mybir

ALU = mybir.AluOpType
ACT = mybir.ActivationFunctionType
F32 = mybir.dt.float32
F32R = mybir.dt.float32r
BF16 = mybir.dt.bfloat16

ARENA = 207360
D = 1024
KB = D // 128
SEQ, DEC, PAST = 1024, 64, 256
TOK = SEQ + DEC
KEYS = SEQ + PAST + DEC
NT = 9
NH_D, NH_S, NH_I, DH = 4, 8, 4, 64
FF = 2816
NEG = -1.0e30
LOW = -3.0e38
EPS = 1e-6
LAM_INIT = 0.8 - 0.6 * math.exp(-0.0)
SCALE = DH ** -0.5
BUCKETS, MAXD = 32, 256
NREL = 1152
CHUNKS = [(0, 352), (352, 352), (704, 384)]

BLOCKS = [("iq", 0, 2304, 128), ("ik", 0, 2560, 68), ("iq", 1, 2432, 128),
          ("dk", 0, 512, 128), ("sk", 0, 2048, 128), ("dk", 1, 640, 128), ("sv", 0, 2176, 128),
          ("dk", 2, 768, 128), ("dv", 0, 1024, 128), ("dk", 3, 896, 128), ("dv", 1, 1152, 128),
          ("dq", 0, 0, 128), ("dv", 2, 1280, 128), ("dq", 1, 128, 128), ("dv", 3, 1408, 128),
          ("dq", 2, 256, 128), ("dq", 3, 384, 128),
          ("sq", 0, 1536, 128), ("sq", 1, 1664, 128), ("sq", 2, 1792, 128), ("sq", 3, 1920, 128)]
NB = len(BLOCKS)
NATURAL = [b for b, blk in enumerate(BLOCKS) if blk[0] in ("ik", "dk", "sk", "sv", "dv")]
QBLOCKS = [b for b, blk in enumerate(BLOCKS) if blk[0] in ("dq", "sq")]
TOPK_TILES = list(range(2, NT))
ADA_W = 256
N_ADA = 6 * D // ADA_W
ADA_FIRST = 2 * D // ADA_W


def rows_of(t):
    return 128 if t < 8 else DEC


def nkeys(t):
    return 128 * (t + 1) if t < 8 else PAST + DEC


def key0(t):
    return 0 if t < 8 else SEQ


def key_blocks(t):
    return [(o, min(128, nkeys(t) - o)) for o in range(0, nkeys(t), 128)]


WORK0 = {}
_o = 0
for _t in TOPK_TILES:
    WORK0[_t] = _o
    _o += nkeys(_t)
WORK_N = _o


def rounds_of(t):
    return min(256, SEQ // 4) // 8 if t < 8 else min(256, (PAST + DEC) // 4) // 8


def dots_tile(b):
    t = b - 1
    return t if b >= 3 and t < NT else None


def ada_after(b):
    return [ADA_FIRST + 2 * (b - 11), ADA_FIRST + 2 * (b - 11) + 1] if 11 <= b < 19 else []


def ada_slot(j):
    return j % 4 if j < ADA_FIRST else j % 2


def ada_turn(j):
    same = [i for i in range(j) if ada_slot(i) == ada_slot(j)]
    return len(same) + 1, (same[-1] if same else None)


LAST = NT - 1
TAIL_OUT = {1: 0, 2: 1}
TAIL_RESIDUAL, TAIL_SQUARE, TAIL_RMS, TAIL_WEIGHTS, TAIL_STORE = 3, 4, 5, 4, 8
EARLY = {5: 0, 8: 1}
FGROUPS = FF // 256
YBANKS = 3
PAIRS = 2
NSTEPS = 8 * NT
SLOTS = NSTEPS + 3
P_ROUNDS = 119


def sparse(s):
    return s % 8 >= 4


def prob_groups(s):
    n = len(key_blocks(s // 8))
    return [("p", s, m, q) for m in range(2 if sparse(s) else 1) for q in range((n + 3) // 4)]


def prob_part(slot, part):
    if not 2 <= slot < NSTEPS + 2:
        return []
    groups = prob_groups(slot - 2)
    return groups[:2] if part == 0 else groups[2:]


def out_half(slot):
    t, half = divmod(slot - 11, 8)
    return (t, half) if 0 <= t < NT and half < 2 else None


def tile_at(slot, lag):
    t, rest = divmod(slot - lag, 8)
    return t if 0 <= t < NT and rest == 0 else None


def p_rounds(t):
    return max(0, min(rounds_of(t), P_ROUNDS - sum(rounds_of(u) for u in TOPK_TILES if u < t)))


def topk_schedule():
    plan = [[] for _ in range(NSTEPS)]
    halves = {t: [(t, h) for _ in range(rounds_of(t) - p_rounds(t)) for h in range(2)] for t in TOPK_TILES}
    last = NT - 1
    for todo, first, end in ((sum((halves[t] for t in TOPK_TILES if t != last), []), 0, 8 * (last - 1) - 1),
                             (halves[last], 8 * (last - 1) - 1, 8 * last - 1)):
        weights = [nkeys(slot // 8) + 256 for slot in range(first, end)]
        done = 0
        for i, slot in enumerate(range(first, end)):
            upto = -(-len(todo) * sum(weights[:i + 1]) // sum(weights))
            plan[slot] += todo[done:upto]
            done = upto
    for t in TOPK_TILES:
        assert not any(u == t for slot in range(8 * t, NSTEPS) for u, _ in plan[slot])
    return plan


TOPK_PLAN = topk_schedule()


def topk_part(slot, point):
    todo = TOPK_PLAN[slot] if slot < NSTEPS else []
    return todo[len(todo) * point // 4:len(todo) * (point + 1) // 4]


T_ORDER = [("params",)]
T_ORDER += [("x", t, half) for t in range(NT) for half in range(2)]
T_ORDER += [("cache", j) for j in range(3)]
for _b in range(NB):
    if _b - 1 in NATURAL:
        T_ORDER += [("nat", _b - 1, q) for q in range(3)]
T_ORDER += [("gates",)]
for _s in range(NSTEPS + 3):
    if 2 <= _s < NSTEPS + 2:
        T_ORDER += prob_groups(_s - 2)
    if _s >= 3:
        T_ORDER += [("o", _s - 3)]
T_ORDER += [("f", t, half) for t in range(NT) for half in range(2)]
T_INDEX = {k: i for i, k in enumerate(T_ORDER)}


def bias_row_onehot():
    rel = 127 - np.arange(NREL)
    nb = BUCKETS // 2
    exact = nb // 2
    n = np.abs(rel)
    nf = np.maximum(n, 1).astype(np.float32)
    large = exact + (np.log(nf / np.float32(exact)) / np.float32(math.log(MAXD / exact))
                     * np.float32(nb - exact)).astype(np.int32)
    bucket = np.where(rel > 0, nb, 0) + np.where(n < exact, n, np.minimum(large, nb - 1))
    return (bucket[None, :] == np.arange(BUCKETS)[:, None]).astype(np.float32)


def build(nc, I, O):
    ctx = ExitStack()
    with ctx:
        def sb(name, shape, dt=F32):
            return ctx.enter_context(nc.sbuf_tensor(name, shape, dt))

        def ps(name, cols, dt=F32):
            return ctx.enter_context(nc.psum_tensor(name, [128, cols], dt))

        def sem(name):
            return ctx.enter_context(nc.semaphore(name))

        ident = sb("ident", [128, 128])
        identb = sb("identb", [128, 128], BF16)
        maskb = sb("maskb", [128, 128], BF16)
        prow = sb("prow", [97, 128])
        cols = sb("cols", [128, 97])
        csil = sb("csil", [128, KB, 2])
        modT = sb("modT", [128, 48, 2])
        scaleA = sb("scaleA", [128, 2, KB, 2])
        gates = sb("gates", [128, 2, 2, KB])
        gaterow = sb("gaterow", [32, 128])
        subln = sb("subln", [128, 1])
        lamv = sb("lamv", [128, 4, DH])
        lam = sb("lam", [128, 8])
        iwn = sb("iwn", [128, NT, NH_I])
        stat = sb("stat", [128, 64])
        top8 = sb("top8", [128, 8])
        minus_half = sb("minus_half", [128, 1])
        spare = sb("spare", [128, 2])

        base = [0]
        arena = ctx.enter_context(nc.sbuf_tensor("arena", [128, ARENA // 4], F32))
        A0 = arena_offset(nc, arena)

        def place(name, shape, dt, off):
            size = int(np.prod(shape[1:])) * (2 if dt == BF16 else 4)
            assert off + size <= ARENA, (name, off + size)
            t = nc.alloc_sbuf_tensor_at(name, shape, dt, offset=A0 + off)
            base[0] = off + size
            return t

        def then(name, shape, dt=F32):
            return place(name, shape, dt, (base[0] + 31) // 32 * 32)

        kT = place("kT", [128, NH_D, KEYS], F32, 0)
        skD = then("skD", [128, 2, KEYS])
        work = then("work", [128, WORK_N])
        shared_end = base[0]
        hTh = then("hTh", [128, KB, TOK], F32R)
        hTl = then("hTl", [128, KB, TOK], F32R)
        ada = then("ada", [128, 2, KB, ADA_W])
        wraw = then("wraw", [128, 2, KB, 128])
        wh = then("wh", [128, 2, KB, 128], F32R)
        wl = then("wl", [128, 2, KB, 128], F32R)
        ada_more = place("ada_more", [128, 2, KB, ADA_W], F32, base[0] - 2 * 8 * KB * 128)
        iqT = then("iqT", [128, 2, TOK])
        ikD = then("ikD", [128, KEYS])
        late = base[0]
        qst = then("qst", [128, 2, TOK])
        relu = then("relu", [128, 2, 1024])
        late2 = base[0]
        vT = then("vT", [128, TOK])
        nat = then("nat", [128, 2, NT, 128])
        adarow = then("adarow", [2, ADA_W])
        xin = place("xin", [128, 2, D], F32, late)
        xn = then("xn", [128, 2, D])
        vt = place("vt", [128, 2, KB, 128], F32, late2 + 32)
        work_off = 4 * (NH_D * KEYS + 2 * KEYS)
        cachek = place("cachek", [128, 2, 704], F32, work_off)
        onehot = then("onehot", [BUCKETS, NREL])
        rrow = then("rrow", [12, NREL])
        tab = then("tab", [BUCKETS, 12])

        vsb = place("vsb", [128, 11, 640], F32, shared_end)
        ering_off = (base[0] + 31) // 32 * 32
        ering = then("ering", [128, 4, 1024])
        sc = then("sc", [128, 3, 2, 1024])
        aT = then("aT", [128, 2, 8, 128])
        wout = then("wout", [128, KB, D])
        oT = then("oT", [128, 2, KB, 128])
        qt = then("qt", [128, 2, 8, 128])
        keep = then("keep", [128, 2, 1024], BF16)
        msb = then("msb", [128, D])
        junk = then("junk", [128, D])
        xt = then("xt", [128, 2, D])
        gate1 = then("gate1", [128, 2, D])
        ob = then("ob", [128, 2, 128])
        obj = then("obj", [128, 128])
        nmax = sb("nmax", [128, 4, 2])
        rsum = sb("rsum", [128, 4, 2])
        rinv = sb("rinv", [128, 4, 2])
        rlam = sb("rlam", [128, 4])
        oss = sb("oss", [128, 2])
        mss = sb("mss", [128, 2, NT])

        h2h = place("h2h", [128, KB, TOK], F32R, 0)
        h2l = then("h2l", [128, KB, TOK], F32R)
        yacc = then("yacc", [128, NT, D])
        yacc_end = base[0]
        graw = then("graw", [128, 2, KB, 256])
        gh = then("gh", [128, 2, KB, 256], F32R)
        gl = then("gl", [128, 2, KB, 256], F32R)
        draw = then("draw", [128, 2, D])
        dh = then("dh", [128, 2, D], F32R)
        dl = then("dl", [128, 2, D], F32R)
        ah = then("ah", [128, 2, TOK], F32R)
        al = then("al", [128, 2, TOK], F32R)
        sg = then("sg", [128, 2, 384])
        hv = then("hv", [128, 2, 384])
        x2in = place("x2in", [128, 2, D], F32, ering_off)
        x2n = then("x2n", [128, 2, D])
        v2 = then("v2", [128, 2, KB, 128])
        assert base[0] <= yacc_end
        gate2 = place("gate2", [128, 2, D], F32, 0)
        x2r = then("x2r", [128, NT, D])

        S = [ps(f"S{m}", 1024) for m in range(2)]
        T = [ps(f"T{m}", 512) for m in range(2)]
        PJ = [ps(f"PJ{m}", 512) for m in range(2)]
        YB = [T[0], T[1], PJ[0]]

        q_dram = nc.dram_tensor("q_scratch", [8, 128, TOK], F32, kind="Internal").ap()
        r_dram = nc.dram_tensor("r_scratch", [12, NREL], F32, kind="Internal").ap()
        g_dram = nc.dram_tensor("g_scratch", [32, 128], F32, kind="Internal").ap()

        x2_dram = nc.dram_tensor("x2_scratch", [TOK, D], F32, kind="Internal").ap()

        ld_x2 = [sem(f"ld_x2{i}") for i in range(2)]
        x2n_ready = sem("x2n_ready")
        hi2_ready = sem("hi2_ready")
        lo2_ready = [sem(f"lo2_ready{i}") for i in range(2)]
        yacc_zero = sem("yacc_zero")
        ld_g = [sem(f"ld_g{i}") for i in range(2)]
        ld_d = [sem(f"ld_d{i}") for i in range(2)]
        g_hi = sem("g_hi")
        g_lo = sem("g_lo")
        d_hi = sem("d_hi")
        d_lo = sem("d_lo")
        gu_done = sem("gu_done")
        silu_out = sem("silu_out")
        hv_ready = sem("hv_ready")
        a_hi = sem("a_hi")
        a_lo = sem("a_lo")
        y_done = sem("y_done")
        y_added = sem("y_added")
        ld_gate2 = sem("ld_gate2")
        ld_x2r = [sem(f"ld_x2r{i}") for i in range(NT)]
        y_scaled = sem("y_scaled")
        y_squared = sem("y_squared")
        y_rms = sem("y_rms")
        y_ready = sem("y_ready")
        y_stored = sem("y_stored")

        ld_vfix = sem("ld_vfix")
        ld_v = [sem(f"ld_v{i}") for i in range(2)]
        ld_e = [sem(f"ld_e{i}") for i in range(4)]
        ld_q7 = sem("ld_q7")
        ld_q = [sem(f"ld_q{i}") for i in range(2)]
        ld_xt = [sem(f"ld_xt{i}") for i in range(2)]
        ld_wout = sem("ld_wout")
        ld_gate1 = sem("ld_gate1")
        lam_ready = sem("lam_ready")
        qk_done = sem("qk_done")
        biased = sem("biased")
        exp_done = sem("exp_done")
        combined = sem("combined")
        pv_done = sem("pv_done")
        o_read = sem("o_read")
        o_squared = sem("o_squared")
        o_rms = sem("o_rms")
        o_ready = sem("o_ready")
        keep_ready = sem("keep_ready")
        m_done = sem("m_done")
        m_out = sem("m_out")
        m_squared = sem("m_squared")
        m_rms = sem("m_rms")
        m_scaled = sem("m_scaled")
        x2_ready = sem("x2_ready")
        x2_squared = sem("x2_squared")
        x2_rms = sem("x2_rms")
        x2_stored = sem("x2_stored")

        ld_params = sem("ld_params")
        ld_lam = sem("ld_lam")
        ld_tab = sem("ld_tab")
        ld_cache = sem("ld_cache")
        ld_ada = [sem(f"ld_ada{i}") for i in range(4)]
        ld_x = [sem(f"ld_x{i}") for i in range(2)]
        ld_w = [sem(f"ld_w{i}") for i in range(2)]
        consts = sem("consts")
        vchain = sem("vchain")
        t_filled = [sem(f"t_filled{i}") for i in range(2)]
        t_freed = [sem(f"t_freed{i}") for i in range(2)]
        silu_done = sem("silu_done")
        mod_ready = sem("mod_ready")
        ada_used = sem("ada_used")
        ada_out = sem("ada_out")
        ada_cols = sem("ada_cols")
        x_squared = sem("x_squared")
        xn_ready = sem("xn_ready")
        rms_ready = sem("rms_ready")
        pchain = sem("pchain")
        hi_ready = sem("hi_ready")
        lo_ready = [sem(f"lo_ready{i}") for i in range(2)]
        w_hi = sem("w_hi")
        w_lo = sem("w_lo")
        chunk_done = sem("chunk_done")
        chunk_out = sem("chunk_out")
        nat_stored = [sem(f"nat_stored{i}") for i in range(2)]
        q_stored = [sem(f"q_stored{i}") for i in range(2)]
        r_made = sem("r_made")
        r_out = sem("r_out")
        r_stored = sem("r_stored")
        dots_done = sem("dots_done")
        relu_done = sem("relu_done")
        score_acc = sem("score_acc")
        gates_ready = sem("gates_ready")
        g_stored = sem("g_stored")

        def ada_in(j):
            slot = ada_slot(j)
            return ada[:, slot, :, :] if slot < 2 else ada_more[:, slot - 2, :, :]

        def wait_lows(eng, lows, count):
            for i in range(2):
                if (count + 1 - i) // 2:
                    eng.wait_ge(lows[i], (count + 1 - i) // 2)

        def t_wait_free(eng, key):
            g = T_INDEX[key]
            if g >= 2:
                eng.wait_ge(t_freed[g % 2], g // 2)
            return T[g % 2]

        def t_wait_full(eng, key):
            g = T_INDEX[key]
            eng.wait_ge(t_filled[g % 2], g // 2 + 1)
            return T[g % 2]

        def t_wait_freed(eng, key):
            g = T_INDEX[key]
            eng.wait_ge(t_freed[g % 2], g // 2 + 1)

        def filled(key):
            return t_filled[T_INDEX[key] % 2]

        def freed(key):
            return t_freed[T_INDEX[key] % 2]

        def low_rows(eng, highs, lows, low, rows, high, t):
            r, c = rows_of(t), 128 * t
            eng.wait_ge(highs, t + 1)
            eng.tensor_tensor(low[:, :, c:c + r], rows[:, t % 2, :, 0:r], high[:, :, c:c + r].bitcast(F32),
                              ALU.subtract).then_inc(lows[t % 2], 1)

        def key_pieces(c0, n):
            if c0 + n <= SEQ:
                return [(0, c0, n)]
            return [(0, c0, SEQ - c0), (SEQ - c0, SEQ + PAST, c0 + n - SEQ)]

        def nat_source(b, t):
            kind, h, _, w = BLOCKS[b]
            if kind == "dk":
                c = 128 * t if t < 8 else SEQ + PAST
                return kT[:, h, c:c + rows_of(t)]
            return vT[0:w, 128 * t:128 * t + rows_of(t)]

        nat_slot = {b: i % 2 for i, b in enumerate(NATURAL)}
        nat_count = {b: i // 2 for i, b in enumerate(NATURAL)}
        q_slot = {b: i % 2 for i, b in enumerate(QBLOCKS)}
        q_count = {b: i // 2 for i, b in enumerate(QBLOCKS)}

        def nat_outputs(b):
            kind, h, _, _ = BLOCKS[b]
            if kind == "dk":
                return I_w(O["dk_p"], h), O["dk_s"][:, h, :], 128
            if kind == "dv":
                return I_w(O["dv_p"], h), O["dv_s"][:, h, :], 128
            name = {"sk": "sk", "sv": "sv", "ik": "ik"}[kind]
            return O[name + "_p"].rearrange("(t p) e -> p t e", p=128), O[name + "_s"], 64 if kind == "ik" else 128

        def I_w(out, h):
            return out.rearrange("(t p) h e -> p t h e", p=128)[:, :, h, :]

        def y_rows(t):
            return slice(0, 128) if t < 8 else slice(64, 128)

        def y_cols(t):
            return slice(128 * t, 128 * t + 128) if t < 8 else slice(TOK - 128, TOK)

        def store_y(sp, t):
            sp.wait_ge(y_ready, t + 1)
            dst = O["y_p"][128 * t:128 * t + 128, :] if t < 8 else O["y_s"]
            sp.dma_start(dst, yacc[y_rows(t), t, :]).then_inc(y_stored, 16)

        def step(s):
            t = s // 8
            return t, s % 8, rows_of(t), nkeys(t)

        def bias_slot(s, m):
            t, i, _, _ = step(s)
            return 12 * t + (i if i < 4 else 4 + 2 * (i - 4) + m)

        def biased_by(e):
            t, j = divmod(e, 12)
            return 2 * (8 * t + j) + 2 if j < 4 else 2 * (8 * t + 4 + (j - 4) // 2) + (j - 4) % 2 + 1

        def diff_count(s):
            return 4 * (s // 8) + min(s % 8 + 1, 4)

        block = ctx.enter_context(nc.Block())

        @block.sync
        def _(sp):
            for i, (name, r0, n) in enumerate(PARAM_ROWS):
                sp.dma_start(prow[r0:r0 + n, :], I[name].rearrange("(r c) -> r c", c=128)).then_inc(ld_params, 16)

            def load_ada(j):
                slot, last = ada_slot(j), ada_turn(j)[1]
                if last is not None:
                    sp.wait_ge(ada_used, last + 1)
                sp.dma_start(ada_in(j), I["w_ada"].rearrange("(k p) n -> p k n", p=128)
                             [:, :, ADA_W * j:ADA_W * (j + 1)]).then_inc(ld_ada[slot], 16)

            def load_x(t):
                if t >= 2:
                    sp.wait_ge(xn_ready, t - 1)
                src = I["x_p"][128 * t:128 * (t + 1), :] if t < 8 else I["x_s"]
                sp.dma_start(xin[0:rows_of(t), t % 2, :], src).then_inc(ld_x[t % 2], 16)

            def load_w(b):
                if b >= 2:
                    sp.wait_ge(w_lo, b - 1)
                _, _, c, n = BLOCKS[b]
                sp.dma_start(wraw[:, b % 2, :, 0:n], I["w_in"].rearrange("(k p) n -> p k n", p=128)
                             [:, :, c:c + n]).then_inc(ld_w[b % 2], 16)

            load_x(0)
            load_x(1)
            for j in range(4):
                load_ada(j)
            for i, name in enumerate(("lq1", "lk1", "lq2", "lk2")):
                sp.dma_start(lamv[:, i, :], I[name].rearrange("(a n) -> a n", a=1).broadcast_to([128, DH])
                             ).then_inc(ld_lam, 16)
            sp.dma_start(tab[:, :], I["tab"]).then_inc(ld_tab, 16)
            sp.dma_start(onehot[:, :], I["onehot"]).then_inc(ld_tab, 16)
            for j in range(4, ADA_FIRST):
                load_ada(j)
            for t in range(2, 4):
                load_x(t)
            load_w(0)
            load_w(1)
            for t in range(4, NT):
                load_x(t)
            for i in range(2):
                r = slice(128 * i, 128 * i + 128)
                sp.dma_start(cachek[:, i, 0:512], I["c_dk"][r].rearrange("p h e -> p (h e)")).then_inc(ld_cache, 16)
                sp.dma_start(cachek[:, i, 512:640], I["c_sk"][r].rearrange("p h e -> p (h e)")
                             ).then_inc(ld_cache, 16)
                sp.dma_start(cachek[:, i, 640:704], I["c_ik"][r]).then_inc(ld_cache, 16)

            def store_nat(b):
                prompt, sample, w = nat_outputs(b)
                for q in range(3):
                    t_wait_freed(sp, ("nat", b, q))
                s = nat_slot[b]
                sp.dma_start(prompt, nat[:, s, 0:8, 0:w]).then_inc(nat_stored[s], 16)
                sp.dma_start(sample, nat[0:DEC, s, 8, 0:w]).then_inc(nat_stored[s], 16)

            sp.wait_ge(r_out, 3)
            sp.dma_start(r_dram, rrow[:, :]).then_inc(r_stored, 16)
            def load_q(t, i0, i1):
                r = rows_of(t)
                sp.dma_start(qt[:, t % 2, i0:i1, 0:r], q_dram[i0:i1, :, 128 * t:128 * t + r]
                             .rearrange("b p t -> p b t")).then_inc(ld_q[t % 2] if i0 == 0 else ld_q7, 16)

            for b in range(NB):
                if b == NB - 1:
                    sp.wait_ge(score_acc, NH_I * len(TOPK_TILES))
                    sp.wait_ge(q_stored[q_slot[b - 1]], 16 * (q_count[b - 1] + 1))
                    sp.wait_ge(q_stored[q_slot[b - 2]], 16 * (q_count[b - 2] + 1))
                    load_q(0, 0, 7)
                if b + 2 < NB:
                    load_w(b + 2)
                for j in ada_after(b + 1):
                    load_ada(j)
                if b in QBLOCKS:
                    sp.wait_ge(chunk_out, 3 * (b + 1))
                    sp.dma_start(q_dram[QBLOCKS_POS[b]], qst[:, q_slot[b], :]).then_inc(q_stored[q_slot[b]], 16)
                if b - 1 in NATURAL:
                    store_nat(b - 1)
            for s in range(2):
                sp.wait_ge(nat_stored[s], 32 * len([b for b in NATURAL if nat_slot[b] == s]))
                sp.wait_ge(q_stored[s], 16 * len(QBLOCKS) // 2)
            sp.wait_ge(r_stored, 16)
            sp.wait_ge(score_acc, NH_I * len(TOPK_TILES))
            sp.wait_ge(ada_used, N_ADA)
            sp.wait_ge(chunk_done, 3 * NB)

            def load_e(e):
                t, j = divmod(e, 12)
                if e >= 4:
                    sp.wait_ge(biased, biased_by(e - 4))
                r, n = rows_of(t), nkeys(t)
                src = bass.AP(tensor=r_dram.tensor, offset=j * NREL + (0 if t < 8 else 64), ap=[[1, r], [1, n]])
                sp.dma_start(ering[0:r, e % 4, 0:n], src).then_inc(ld_e[e % 4], 16)

            def load_tile(t):
                r = rows_of(t)
                if t >= 2:
                    sp.wait_ge(qk_done, 16 * (t - 1))
                if t:
                    load_q(t, 0, 8)
                if t < 8:
                    v = vsb[:, t, :]
                    rows = slice(128 * t, 128 * t + 128)
                    sp.dma_start(v[:, 0:512], O["dv_p"][rows].rearrange("p h e -> p (h e)")).then_inc(ld_v[t % 2], 16)
                    sp.dma_start(v[:, 512:640], O["sv_p"][rows]).then_inc(ld_v[t % 2], 16)

            def load_rows(t):
                r = rows_of(t)
                if t >= 2:
                    sp.wait_ge(x2_ready, t - 1)
                src = I["x_p"][128 * t:128 * (t + 1), :] if t < 8 else I["x_s"]
                sp.dma_start(xt[0:r, t % 2, :], src).then_inc(ld_xt[t % 2], 16)

            load_e(0)
            load_e(1)
            load_q(0, 7, 8)
            load_tile(0)
            load_e(2)
            load_e(3)
            t_wait_freed(sp, ("gates",))
            sp.dma_start(g_dram, gaterow[:, :]).then_inc(g_stored, 16)
            load_tile(1)
            load_rows(0)
            load_rows(1)
            for i in range(2):
                rows = slice(128 * i, 128 * i + 128)
                sp.dma_start(vsb[:, 8 + i, 0:512], I["c_dv"][rows].rearrange("p h e -> p (h e)")).then_inc(ld_vfix, 16)
                sp.dma_start(vsb[:, 8 + i, 512:640], I["c_sv"][rows].rearrange("p h e -> p (h e)")
                             ).then_inc(ld_vfix, 16)
            sp.dma_start(vsb[0:DEC, 10, 0:512], O["dv_s"].rearrange("p h e -> p (h e)")).then_inc(ld_vfix, 16)
            sp.dma_start(vsb[0:DEC, 10, 512:640], O["sv_s"]).then_inc(ld_vfix, 16)

            def store_x2(t):
                r = rows_of(t)
                sp.wait_ge(x2_ready, t + 1)
                sp.dma_start(x2_dram[128 * t:128 * t + r, :], msb[0:r, :]).then_inc(x2_stored, 16)

            for e in range(4, 12 * NT):
                load_e(e)
                t, j = divmod(e, 12)
                if e - 4 < KB:
                    k = e - 4
                    sp.dma_start(wout[:, k, :], I["w_out"][128 * k:128 * k + 128, :]).then_inc(ld_wout, 16)
                if e == 4 + KB:
                    sp.wait_ge(g_stored, 16)
                    for g in range(2):
                        sp.dma_start(gate1[:, g, :], g_dram[8 * g:8 * g + 8, :].rearrange("(a k) c -> a (k c)", a=1)
                                     .broadcast_to([128, D])).then_inc(ld_gate1, 16)
                if j == 4 and 1 <= t < NT - 1:
                    load_tile(t + 1)
                if j == 10 and t >= 1:
                    store_x2(t - 1)
                    if t < NT - 1:
                        load_rows(t + 1)
            w_gate_up = I["w_gu"].rearrange("(k p) n -> p k n", p=128)

            def load_x2(t):
                r = rows_of(t)
                sp.wait_ge(x2_stored, 16 * (t + 1))
                if t >= 2:
                    sp.wait_ge(x2n_ready, t - 1)
                sp.dma_start(x2in[0:r, t % 2, :], x2_dram[128 * t:128 * t + r, :]).then_inc(ld_x2[t % 2], 16)

            def load_gu(slot, j):
                for part in range(2):
                    sp.dma_start(graw[:, slot, :, 128 * part:128 * part + 128],
                                 w_gate_up[:, :, bass.ds(FF * part + 128 * j, 128)]).then_inc(ld_g[slot], 16)

            def load_down(slot, j):
                sp.dma_start(draw[:, slot, :], I["w_down"][bass.ds(128 * j, 128), :]).then_inc(ld_d[slot], 16)

            sp.wait_ge(biased, 2 * NSTEPS)
            load_x2(0)
            load_x2(1)
            for t in range(2, NT):
                if t == 4:
                    sp.wait_ge(pv_done, NSTEPS)
                    load_gu(0, 0)
                    load_gu(1, 1)
                if t == TAIL_STORE:
                    store_x2(NT - 1)
                load_x2(t)
            load_down(0, 0)
            load_down(1, 1)
            with sp.Fori(0, FGROUPS - 1) as g:
                for slot in range(2):
                    sp.wait_ge(g_lo, 2 * g + slot + 1)
                    load_gu(slot, 2 * g + 2 + slot)
                for slot in range(2):
                    sp.wait_ge(d_lo, 2 * g + slot + 1)
                    load_down(slot, 2 * g + 2 + slot)
            sp.wait_ge(gu_done, 6 * FGROUPS)
            for part, rows in enumerate((slice(0, 128), slice(64, 128))):
                n = rows.stop - rows.start
                sp.dma_start(gate2[rows, part, :], g_dram[16 + 8 * part:24 + 8 * part, :]
                             .rearrange("(a k) c -> a (k c)", a=1).broadcast_to([n, D])).then_inc(ld_gate2, 16)
            for t in range(NT):
                rows = y_rows(t)
                sp.dma_start(x2r[rows, t, :], x2_dram[128 * t:128 * t + rows_of(t), :]).then_inc(ld_x2r[t], 16)
            for t in range(NT - 1):
                store_y(sp, t)
            store_y(sp, NT - 1)
            sp.wait_ge(y_stored, 16 * NT)

        @block.gpsimd
        def _(pool):
            pool.memset(ident[:, :], 0.0).then_inc(consts, 1)
            pool.wait_ge(consts, 1)
            pool.affine_select(out=ident[:, :], in_=ident[:, :], compare_op=ALU.not_equal, fill=1.0, base=0,
                               pattern=[[-1, 128]], channel_multiplier=1).then_inc(consts, 1)
            pool.wait_ge(consts, 2)
            pool.tensor_copy(identb[:, :], ident[:, :]).then_inc(consts, 1)
            pool.memset(maskb[:, :], 0.0).then_inc(consts, 1)
            pool.wait_ge(consts, 4)
            pool.memset(maskb[0:64, 64:128], NEG).then_inc(consts, 1)
            pool.memset(minus_half[:, :], -0.5).then_inc(pchain, 1)
            pool.wait_ge(pchain, 1)
            pchain_n = [1]

            def rsqrt_mean(at, n, done, p0=0):
                r = at.shape[0]
                pool.tensor_scalar(at, at, 1.0 / n, EPS, ALU.mult, ALU.add).then_inc(pchain, 1)
                pchain_n[0] += 1
                pool.wait_ge(pchain, pchain_n[0])
                pool.tensor_tensor(at, at, minus_half[p0:p0 + r, :], ALU.pow).then_inc(done, 1)

            def low_w(b):
                pool.wait_ge(w_hi, b + 1)
                n = BLOCKS[b][3]
                pool.tensor_tensor(wl[:, b % 2, :, 0:n], wraw[:, b % 2, :, 0:n],
                                   wh[:, b % 2, :, 0:n].bitcast(F32), ALU.subtract).then_inc(w_lo, 1)

            for t in range(3):
                pool.wait_ge(x_squared, t + 1)
                rsqrt_mean(stat[0:rows_of(t), t:t + 1], D, rms_ready)
            for t in range(NT):
                if t + 3 < NT:
                    pool.wait_ge(x_squared, t + 4)
                    rsqrt_mean(stat[0:rows_of(t + 3), t + 3:t + 4], D, rms_ready)
                if t % 2 == 0:
                    low_rows(pool, hi_ready, lo_ready, hTl, vt, hTh, t)
                if t < 2:
                    low_w(t)
            for b in range(2, NB):
                low_w(b)
            def rms_m(t):
                pool.wait_ge(m_squared, t + 1)
                rsqrt_mean(mss[0:rows_of(t), 0, t:t + 1], D, m_rms)

            def residual(t):
                r = rows_of(t)
                pool.wait_ge(m_scaled, t + 1)
                pool.wait_ge(ld_xt[t % 2], 16 * (t // 2 + 1))
                pool.tensor_tensor(msb[0:r, :], msb[0:r, :], xt[0:r, t % 2, :], ALU.add).then_inc(x2_ready, 1)

            def rms_x2(t):
                pool.wait_ge(x2_squared, t + 1)
                rsqrt_mean(mss[0:rows_of(t), 1, t:t + 1], D, x2_rms)

            for slot in range(SLOTS):
                if 2 <= slot < NSTEPS + 2 and not sparse(slot - 2):
                    s = slot - 2
                    pool.wait_ge(o_squared, diff_count(s))
                    rsqrt_mean(oss[0:rows_of(s // 8), s % 2:s % 2 + 1], 128, o_rms)
                t = tile_at(slot, 12)
                if t is not None:
                    rms_m(t)
                t = tile_at(slot, 13)
                if t is not None:
                    residual(t)
                t = tile_at(slot, 14)
                if t is not None:
                    rms_x2(t)
            def low_gu(slot, count):
                pool.wait_ge(g_hi, count)
                pool.tensor_tensor(gl[:, slot, :, :], graw[:, slot, :, :], gh[:, slot, :, :].bitcast(F32),
                                   ALU.subtract).then_inc(g_lo, 1)

            for t in range(NT):
                if t % 2 == 0:
                    low_rows(pool, hi2_ready, lo2_ready, h2l, v2, h2h, t)
                if t == max(TAIL_OUT):
                    rms_m(LAST)
                if t == TAIL_RESIDUAL:
                    residual(LAST)
                if t == TAIL_RMS:
                    rms_x2(LAST)
                if t == TAIL_WEIGHTS + 1:
                    low_gu(0, 1)

            def ffn_pool(g, more):
                for slot in range(2):
                    pool.wait_ge(d_hi, 2 * g + slot + 1)
                    pool.tensor_tensor(dl[:, slot, :], draw[:, slot, :], dh[:, slot, :].bitcast(F32),
                                       ALU.subtract).then_inc(d_lo, 1)
                for slot in range(2):
                    for c, (c0, n) in enumerate(CHUNKS):
                        u = 3 * slot + c
                        pool.wait_ge(a_hi, 6 * g + u + 1)
                        pool.tensor_tensor(al[:, slot, c0:c0 + n], hv[:, u % 2, 0:n],
                                           ah[:, slot, c0:c0 + n].bitcast(F32), ALU.subtract).then_inc(a_lo, 1)
                    if more:
                        low_gu(slot, 2 * g + 2 + slot + 1)

            low_gu(1, 2)
            pool.memset(spare[:, 0:1], 0.0).then_inc(a_lo, 1)
            pool.memset(spare[:, 1:2], 0.0).then_inc(a_lo, 1)
            wait_lows(pool, lo2_ready, NT)
            pool.memset(yacc[:, :, :], 0.0).then_inc(yacc_zero, 1)
            with pool.Fori(0, FGROUPS - 1) as g:
                ffn_pool(g, True)
            ffn_pool(FGROUPS - 1, False)
            def add_residual(t):
                rows = y_rows(t)
                pool.wait_ge(y_scaled, t + 1)
                pool.wait_ge(ld_x2r[t], 16)
                pool.tensor_tensor(yacc[rows, t, :], yacc[rows, t, :], x2r[rows, t, :], ALU.add).then_inc(y_ready, 1)

            for t in range(NT):
                pool.wait_ge(y_squared, t + 1)
                if t == NT - 1:
                    pool.wait_ge(y_rms, t)
                    pool.wait_ge(y_ready, t - 1)
                rsqrt_mean(mss[y_rows(t), 0, t:t + 1], D, y_rms, y_rows(t).start)
                if t == NT - 1:
                    pool.wait_ge(y_rms, NT)
                if t:
                    add_residual(t - 1)
            pool.wait_ge(y_ready, NT - 1)
            add_residual(NT - 1)

        @block.scalar
        def _(act):
            t_wait_freed(act, ("params",))
            nc.scalar.activation(csil[:, :, :], cols[:, 0:16].rearrange("p (g k) -> p k g", g=2), ACT.Silu
                                 ).then_inc(silu_done, 1)
            nc.scalar.activation(subln[:, :], cols[:, 96:97], ACT.Copy, scale=1.0 - LAM_INIT).then_inc(silu_done, 1)

            def split_w(b):
                act.wait_ge(ld_w[b % 2], 16 * (b // 2 + 1))
                if b == 0:
                    act.wait_ge(ada_used, ADA_FIRST)
                if b >= 2:
                    act.wait_ge(chunk_done, 3 * (b - 1))
                n = BLOCKS[b][3]
                nc.scalar.activation(wh[:, b % 2, :, 0:n], wraw[:, b % 2, :, 0:n], ACT.Copy).then_inc(w_hi, 1)

            def square(t):
                r = rows_of(t)
                act.wait_ge(ld_x[t % 2], 16 * (t // 2 + 1))
                if t:
                    act.wait_ge(x_squared, t)
                nc.scalar.activation(S[1][0:r, :], xin[0:r, t % 2, :], ACT.Square, accum_out=stat[0:r, t:t + 1]
                                     ).then_inc(x_squared, 1)

            def modulate_half(key, dst, norm, t):
                g, r = int(t == 8), rows_of(t)
                bank = t_wait_full(act, key)
                for j in range(4):
                    k = 4 + j
                    last = nc.scalar.activation(dst[:, t % 2, k, 0:r], bank[:, 128 * j:128 * j + r], ACT.Identity,
                                                scale=scaleA[:, norm, k, g:g + 1],
                                                bias=modT[:, 24 * norm + k, g:g + 1])
                last.then_inc(freed(key), 1)

            def high_part(t):
                r, c = rows_of(t), 128 * t
                if t == 0:
                    act.wait_ge(mod_ready, 1)
                if t >= 2:
                    act.wait_ge(lo_ready[t % 2], t // 2)
                modulate_half(("x", t, 1), vt, 0, t)
                for half in range(2):
                    t_wait_freed(act, ("x", t, half))
                nc.scalar.activation(hTh[:, :, c:c + r], vt[:, t % 2, :, 0:r], ACT.Copy).then_inc(hi_ready, 1)

            def row_out(j):
                act.wait_ge(ada_used, j + 1)
                if j:
                    act.wait_ge(ada_cols, j)
                nc.scalar.activation(adarow[:, :], S[0][0:2, 512 * (j % 2):512 * (j % 2) + ADA_W], ACT.Copy
                                     ).then_inc(ada_out, 1)

            def chunk_evac(b, c):
                kind, h, _, w = BLOCKS[b]
                c0, n = CHUNKS[c]
                i = 3 * b + c
                bank = PJ[i % 2]
                act.wait_ge(chunk_done, i + 1)
                copy = lambda out, part=slice(0, 128), o=0, m=n, **kw: nc.scalar.activation(
                    out, bank[part, o:o + m], ACT.Copy, **kw)
                if kind == "iq":
                    last = copy(iqT[:, h, c0:c0 + n])
                elif kind == "dk":
                    for o, k, m in key_pieces(c0, n):
                        last = copy(kT[:, h, k:k + m], o=o, m=m)
                elif kind in ("dq", "sq"):
                    if c == 0 and q_count[b] > 0:
                        act.wait_ge(q_stored[q_slot[b]], 16 * q_count[b])
                    last = copy(qst[:, q_slot[b], c0:c0 + n], scale=SCALE)
                else:
                    if kind in ("sk", "ik"):
                        for o, k, m in key_pieces(c0, n):
                            for half in range(2):
                                dst = slice(64 * half, 64 * half + 64)
                                if kind == "sk":
                                    for g in range(2):
                                        copy(skD[dst, g, k:k + m], slice(64 * g, 64 * g + 64), o, m)
                                else:
                                    copy(ikD[dst, k:k + m], slice(0, 64), o, m)
                    if c == 0:
                        prev = [p for p in NATURAL if p < b and BLOCKS[p][0] != "dk"]
                        if prev:
                            t_wait_full(act, ("nat", prev[-1], 2))
                    last = copy(vT[0:w, c0:c0 + n], slice(0, w))
                last.then_inc(chunk_out, 1)

            square(0)
            square(1)
            for j in range(ADA_FIRST):
                row_out(j)
            for i in range(3):
                act.wait_ge(r_made, i + 1)
                nc.scalar.activation(rrow[:, 384 * i:384 * i + 384], PJ[0][0:12, 0:384], ACT.Copy
                                     ).then_inc(r_out, 1)

            split_w(0)
            split_w(1)
            for t in range(NT):
                if t + 2 < NT:
                    square(t + 2)
                high_part(t)
                if t in EARLY:
                    chunk_evac(0, EARLY[t])
            for j in range(3):
                bank = t_wait_full(act, ("cache", j))
                if j < 2:
                    for m in range(2):
                        last = nc.scalar.activation(kT[:, 2 * j + m, SEQ:SEQ + PAST],
                                                    bank[:, 256 * m:256 * m + 256], ACT.Copy)
                    last.then_inc(freed(("cache", j)), 1)
                else:
                    for half in range(2):
                        dst = slice(64 * half, 64 * half + 64)
                        for g in range(2):
                            nc.scalar.activation(skD[dst, g, SEQ:SEQ + PAST], bank[64 * g:64 * g + 64, 0:256],
                                                 ACT.Copy)
                        last = nc.scalar.activation(ikD[dst, SEQ:SEQ + PAST], bank[0:64, 256:512], ACT.Copy)
                    last.then_inc(freed(("cache", j)), 1)
            def nat_out(b):
                s = nat_slot[b]
                w = BLOCKS[b][3]
                for q in range(3):
                    bank = t_wait_full(act, ("nat", b, q))
                    if q == 0 and nat_count[b] > 0:
                        act.wait_ge(nat_stored[s], 32 * nat_count[b])
                    nt, r = (4, 128) if q < 2 else (1, DEC)
                    view = bank[0:r, 0:128 * nt].rearrange("p (t e) -> p t e", e=128)
                    e = 64 if BLOCKS[b][0] == "ik" else 128
                    if BLOCKS[b][0] == "ik":
                        nc.scalar.activation(iwn[0:r, 4 * q:4 * q + nt, :], view[:, :, 64:68], ACT.Copy,
                                             scale=NH_I ** -0.5)
                    nc.scalar.activation(nat[0:r, s, 4 * q:4 * q + nt, 0:e], view[:, :, 0:e], ACT.Copy
                                         ).then_inc(freed(("nat", b, q)), 1)

            for b in range(NB):
                t = dots_tile(b)
                if t is not None:
                    for hh in range(NH_I):
                        u = NH_I * (t - 2) + hh
                        act.wait_ge(dots_done, u + 1)
                        if u >= 2:
                            act.wait_ge(score_acc, u - 1)
                        r, n = rows_of(t), nkeys(t)
                        nc.scalar.activation(relu[0:r, u % 2, 0:n], S[u % 2][0:r, 0:n], ACT.Relu, scale=SCALE
                                             ).then_inc(relu_done, 1)
                for c in range(3):
                    if b or c not in EARLY.values():
                        chunk_evac(b, c)
                if b - 1 in NATURAL:
                    nat_out(b - 1)
                if b + 2 < NB:
                    split_w(b + 2)
                for j in ada_after(b):
                    row_out(j)
            act.wait_ge(lam_ready, 1)
            nc.scalar.activation(lam[:, 2:4], lam[:, 0:2], ACT.Exp).then_inc(lam_ready, 1)
            act_copy = lambda out, in_, **kw: nc.scalar.activation(out, in_, ACT.Copy, **kw)

            def prob_out(s, m, q):
                t, _, r, _ = step(s)
                key = ("p", s, m, q)
                blocks = key_blocks(t)[4 * q:4 * q + 4]
                bank = t_wait_full(act, key)
                if q == 0 and m == 0 and s >= 1:
                    act.wait_ge(pv_done, s)
                full = [b for b in blocks if b[1] == 128]
                last = act_copy(aT[:, m, 4 * q:4 * q + len(full), 0:r],
                                bank[:, 0:128 * len(full)].rearrange("p (j r) -> p j r", r=128)[:, :, 0:r])
                if len(full) < len(blocks):
                    j, w = len(full), blocks[-1][1]
                    last = act_copy(aT[0:w, m, 4 * q + j, 0:r], bank[0:w, 128 * j:128 * j + r])
                last.then_inc(freed(key), 1)

            def head_out(s):
                t, i, r, _ = step(s)
                bank = t_wait_full(act, ("o", s))
                if i == 0 and t >= 2:
                    act.wait_ge(m_done, 2 * (t - 1))
                gain = {} if sparse(s) else {"scale": subln[:, 0:1]}
                act_copy(oT[:, t % 2, i, 0:r], bank[:, 0:r], **gain).then_inc(freed(("o", s)), 1)

            def out_out(t, half):
                r = rows_of(t)
                act.wait_ge(m_done, 2 * t + half + 1)
                if half == 0 and t:
                    act.wait_ge(x2_stored, 16 * t)
                act_copy(msb[0:r, 512 * half:512 * half + 512], PJ[1][0:r, :]).then_inc(m_out, 1)
                if half:
                    act.wait_ge(m_out, 2 * t + 2)
                    if t:
                        act.wait_ge(x2_squared, t)
                    nc.scalar.activation(junk[0:r, :], msb[0:r, :], ACT.Square, accum_out=mss[0:r, 0, t:t + 1]
                                         ).then_inc(m_squared, 1)

            def square_x2(t):
                r = rows_of(t)
                act.wait_ge(x2_ready, t + 1)
                act.wait_ge(m_squared, t + 1)
                nc.scalar.activation(junk[0:r, :], msb[0:r, :], ACT.Square, accum_out=mss[0:r, 1, t:t + 1]
                                     ).then_inc(x2_squared, 1)

            for slot in range(SLOTS):
                for part in range(2):
                    for key in prob_part(slot, part):
                        prob_out(*key[1:])
                if slot < NSTEPS:
                    _, _, r, n = step(slot)
                    for m in range(2):
                        act.wait_ge(biased, 2 * slot + m + 1)
                        p = sc[0:r, slot % 3, m, 0:n]
                        nc.scalar.activation(p, p, ACT.Exp, scale=-1.0, bias=nmax[0:r, slot % 4, m:m + 1],
                                             accum_out=rsum[0:r, slot % 4, m:m + 1]).then_inc(exp_done, 1)
                if 3 <= slot < NSTEPS + 3:
                    head_out(slot - 3)
                if out_half(slot):
                    out_out(*out_half(slot))
                t = tile_at(slot, 14)
                if t is not None:
                    square_x2(t)
            def high_gu(slot, load):
                act.wait_ge(ld_g[slot], 32 * load)
                act_copy(gh[:, slot, :, :], graw[:, slot, :, :]).then_inc(g_hi, 1)

            for t in range(NT):
                r, c = rows_of(t), 128 * t
                if t >= 2:
                    act.wait_ge(lo2_ready[t % 2], t // 2)
                modulate_half(("f", t, 1), v2, 1, t)
                for half in range(2):
                    t_wait_freed(act, ("f", t, half))
                act_copy(h2h[:, :, c:c + r], v2[:, t % 2, :, 0:r]).then_inc(hi2_ready, 1)
                if t in TAIL_OUT:
                    out_out(LAST, TAIL_OUT[t])
                if t == TAIL_SQUARE:
                    square_x2(LAST)
                if t == TAIL_WEIGHTS:
                    high_gu(0, 1)
                    high_gu(1, 1)

            def ffn_act(g, more):
                act.wait_ge(y_added, YBANKS + 18 * g)
                for slot in range(2):
                    act.wait_ge(ld_d[slot], 16 * g + 16)
                    act_copy(dh[:, slot, :], draw[:, slot, :]).then_inc(d_hi, 1)

                def high_hidden(u):
                    slot, c = divmod(u, 3)
                    c0, n = CHUNKS[c]
                    act.wait_ge(hv_ready, PAIRS + 6 * g + u + 1)
                    act_copy(ah[:, slot, c0:c0 + n], hv[:, u % 2, 0:n]).then_inc(a_hi, 1)

                for u in range(6):
                    slot, c = divmod(u, 3)
                    n = CHUNKS[c][1]
                    act.wait_ge(gu_done, 6 * g + u + 1)
                    act.wait_ge(hv_ready, 6 * g + u + 1)
                    nc.scalar.activation(sg[:, u % 2, 0:n], S[u % 2][:, 0:n], ACT.Silu).then_inc(silu_out, 1)
                    if u:
                        high_hidden(u - 1)
                    if more and c == 2:
                        high_gu(slot, g + 2)
                high_hidden(5)

            with act.Fori(0, FGROUPS - 1) as g:
                ffn_act(g, True)
            ffn_act(FGROUPS - 1, False)
            for t in range(NT):
                rows = y_rows(t)
                act.wait_ge(y_added, YBANKS + 18 * (FGROUPS - 1) + 2 * t + 2)
                if t:
                    act.wait_ge(y_squared, t)
                nc.scalar.activation(S[0][rows, :], yacc[rows, t, :], ACT.Square, accum_out=mss[rows, 0, t:t + 1]
                                     ).then_inc(y_squared, 1)

        @block.vector
        def _(dve):
            chain = [0]

            def link(ins):
                chain[0] += 1
                ins.then_inc(vchain, 1)
                dve.wait_ge(vchain, chain[0])

            bank = t_wait_full(dve, ("params",))
            nc.vector.tensor_copy(cols[:, :], bank[:, 0:97]).then_inc(freed(("params",)), 1)
            dve.wait_ge(ld_lam, 64)
            for i in range(2):
                link(nc.vector.tensor_tensor_reduce(out=lamv[:, 2 * i, :], in0=lamv[:, 2 * i, :],
                                                    in1=lamv[:, 2 * i + 1, :], scale=1.0, scalar=0.0, op0=ALU.mult,
                                                    op1=ALU.add, accum_out=lam[:, i:i + 1]))

            def stats(t):
                r = rows_of(t)
                dve.wait_ge(rms_ready, t + 1)
                if t >= 2:
                    t_wait_full(dve, ("x", t - 2, 1))
                nc.vector.tensor_scalar(xn[0:r, t % 2, :], xin[0:r, t % 2, :], stat[0:r, t:t + 1], None, ALU.mult
                                        ).then_inc(xn_ready, 1)

            def modulate(t):
                g, r = int(t == 8), rows_of(t)
                if t >= 2:
                    dve.wait_ge(lo_ready[t % 2], t // 2)
                bank = t_wait_full(dve, ("x", t, 0))
                for k in range(4):
                    last = nc.vector.tensor_scalar(vt[:, t % 2, k, 0:r], bank[:, 128 * k:128 * k + r],
                                                   scaleA[:, 0, k, g:g + 1], modT[:, k, g:g + 1],
                                                   ALU.mult, ALU.add)
                last.then_inc(freed(("x", t, 0)), 1)

            dve.wait_ge(freed(("params",)), 1)
            stats(0)
            stats(1)
            dve.wait_ge(ada_cols, ADA_FIRST)
            link(nc.vector.tensor_tensor(modT[:, 0:16, :], PJ[1][:, 0:32].rearrange("p (j g) -> p j g", g=2),
                                         cols[:, 48:64].rearrange("p (j a) -> p j a", a=1).broadcast_to([128, 16, 2]),
                                         ALU.add))
            link(nc.vector.scalar_tensor_tensor(
                out=scaleA[:, 0, :, :], in0=modT[:, 8:16, :], scalar=1.0,
                in1=cols[:, 16:24].rearrange("p (j a) -> p j a", a=1).broadcast_to([128, KB, 2]),
                op0=ALU.add, op1=ALU.mult))
            nc.vector.tensor_copy(lam[:, 6:7], lam[:, 0:1]).then_inc(mod_ready, 1)
            for t in range(NT):
                if t >= 1 and t + 1 < NT:
                    stats(t + 1)
                modulate(t)
                if t and t % 2 == 0:
                    low_rows(nc.vector, hi_ready, lo_ready, hTl, vt, hTh, t - 1)
            nc.vector.tensor_copy(lam[:, 4:5], lam[:, 0:1]).then_inc(lam_ready, 1)
            for q in range(3):
                t_wait_freed(dve, ("nat", 1, q))
            for t in TOPK_TILES:
                r, n, o = rows_of(t), nkeys(t), WORK0[t]
                for hh in range(NH_I):
                    u = NH_I * (t - 2) + hh
                    dve.wait_ge(relu_done, u + 1)
                    w = iwn[0:r, t, hh:hh + 1]
                    if hh == 0:
                        nc.vector.tensor_scalar(work[0:r, o:o + n], relu[0:r, u % 2, 0:n], w, None, ALU.mult
                                                ).then_inc(score_acc, 1)
                    else:
                        dve.wait_ge(score_acc, u)
                        nc.vector.scalar_tensor_tensor(out=work[0:r, o:o + n], in0=relu[0:r, u % 2, 0:n], scalar=w,
                                                       in1=work[0:r, o:o + n], op0=ALU.mult, op1=ALU.add
                                                       ).then_inc(score_acc, 1)
                if t < 8:
                    dve.wait_ge(score_acc, NH_I * (t - 1))
                    link(nc.vector.memset(work[0:64, o + n - 64:o + n], NEG))

            def topk_half(t, marking):
                r, n, o = rows_of(t), nkeys(t), WORK0[t]
                if not marking:
                    link(nc.vector.max(top8[0:r, :], work[0:r, o:o + n]))
                else:
                    link(nc.vector.match_replace(out=work[0:r, o:o + n], in_to_replace=top8[0:r, :],
                                                 in_values=work[0:r, o:o + n], imm_value=LOW))

            for t in TOPK_TILES:
                for k in range(p_rounds(t)):
                    topk_half(t, 0)
                    topk_half(t, 1)
            dve.wait_ge(ada_cols, N_ADA)
            link(nc.vector.tensor_tensor(modT[:, 16:48, :], S[1][:, 0:64].rearrange("p (j g) -> p j g", g=2),
                                         cols[:, 64:96].rearrange("p (j a) -> p j a", a=1).broadcast_to([128, 32, 2]),
                                         ALU.add))
            link(nc.vector.scalar_tensor_tensor(
                out=scaleA[:, 1, :, :], in0=modT[:, 32:40, :], scalar=1.0,
                in1=cols[:, 24:32].rearrange("p (j a) -> p j a", a=1).broadcast_to([128, KB, 2]),
                op0=ALU.add, op1=ALU.mult))
            for i, (m0, c0) in enumerate(((16, 32), (40, 40))):
                link(nc.vector.tensor_tensor(
                    gates[:, i, :, :].rearrange("p g k -> p k g"), modT[:, m0:m0 + 8, :],
                    cols[:, c0:c0 + 8].rearrange("p (j a) -> p j a", a=1).broadcast_to([128, KB, 2]), ALU.mult))
            nc.vector.tensor_copy(lam[:, 7:8], gates[:, 0, 0, 0:1]).then_inc(gates_ready, 1)
            bank = t_wait_full(dve, ("gates",))
            nc.vector.tensor_copy(gaterow[:, :], bank[0:32, 0:128]).then_inc(freed(("gates",)), 1)
            dve.wait_ge(lam_ready, 2)
            link(nc.vector.scalar_tensor_tensor(out=lam[:, 5:6], in0=lam[:, 2:3], scalar=LAM_INIT, in1=lam[:, 3:4],
                                                op0=ALU.add, op1=ALU.subtract))

            def gated(t):
                r, g = rows_of(t), int(t == 8)
                dve.wait_ge(m_rms, t + 1)
                if t == 0:
                    dve.wait_ge(ld_gate1, 32)
                nc.vector.scalar_tensor_tensor(out=msb[0:r, :], in0=msb[0:r, :], scalar=mss[0:r, 0, t:t + 1],
                                               in1=gate1[0:r, g, :], op0=ALU.mult, op1=ALU.mult
                                               ).then_inc(m_scaled, 1)

            def sums(s):
                r = rows_of(s // 8)
                dve.wait_ge(exp_done, 2 * s + 2)
                link(nc.vector.reciprocal(rinv[0:r, s % 4, :], rsum[0:r, s % 4, :]))
                if not sparse(s):
                    link(nc.vector.scalar_tensor_tensor(out=rlam[0:r, s % 4:s % 4 + 1], in0=rinv[0:r, s % 4, 1:2],
                                                        scalar=lam[0:r, 5:6], in1=rsum[0:r, s % 4, 0:1],
                                                        op0=ALU.mult, op1=ALU.mult))

            def topk_at(slot, point):
                for half in topk_part(slot, point):
                    topk_half(*half)

            for slot in range(SLOTS):
                if 3 <= slot < NSTEPS + 3 and not sparse(slot - 3):
                    s = slot - 3
                    r = rows_of(s // 8)
                    dve.wait_ge(o_rms, diff_count(s))
                    nc.vector.tensor_scalar(ob[0:r, s % 2, :], ob[0:r, s % 2, :], oss[0:r, s % 2:s % 2 + 1], None,
                                            ALU.mult).then_inc(o_ready, 1)
                for m in range(2):
                    if slot < NSTEPS:
                        s = slot
                        t, _, r, n = step(s)
                        dve.wait_ge(qk_done, 2 * s + m + 1)
                        e = bias_slot(s, m)
                        dve.wait_ge(ld_e[e % 4], 16 * (e // 4 + 1))
                        if m == 0 and s >= 3:
                            for key in prob_groups(s - 3)[-2:]:
                                t_wait_full(dve, key)
                        rev = ering[0:r, e % 4, n - 1::-1] if n == 1024 else ering[0:r, e % 4, 0:n][:, ::-1]
                        nc.vector.tensor_tensor_reduce(out=sc[0:r, s % 3, m, 0:n], in0=S[m][0:r, 0:n], in1=rev,
                                                       scale=-1.0, scalar=3.0e38, op0=ALU.add, op1=ALU.min,
                                                       accum_out=nmax[0:r, s % 4, m:m + 1]).then_inc(biased, 1)
                    if m == 0 and 1 <= slot <= NSTEPS:
                        sums(slot - 1)
                    if m == 0 and 1 <= slot <= NSTEPS and not sparse(slot - 1):
                        s = slot - 1
                        _, _, r, n = step(s)
                        nc.vector.scalar_tensor_tensor(out=sc[0:r, s % 3, 0, 0:n], in0=sc[0:r, s % 3, 1, 0:n],
                                                       scalar=rlam[0:r, s % 4:s % 4 + 1], in1=sc[0:r, s % 3, 0, 0:n],
                                                       op0=ALU.mult, op1=ALU.subtract).then_inc(combined, 1)
                    topk_at(slot, m)
                topk_at(slot, 2)
                if 2 <= slot < NSTEPS + 2:
                    s = slot - 2
                    t, i, r, _ = step(s)
                    dve.wait_ge(pv_done, s + 1)
                    if s >= 2:
                        t_wait_full(dve, ("o", s - 2))
                    if sparse(s):
                        for m in range(2):
                            last = nc.vector.tensor_scalar(ob[0:r, s % 2, 64 * m:64 * m + 64],
                                                           PJ[0][0:r, 64 * m:64 * m + 64],
                                                           rinv[0:r, s % 4, m:m + 1], None, ALU.mult)
                        last.then_inc(o_read, 1)
                    else:
                        nc.vector.tensor_scalar(ob[0:r, s % 2, :], PJ[0][0:r, 0:128], rinv[0:r, s % 4, 0:1], -1.0,
                                                ALU.mult, ALU.mult).then_inc(o_read, 1)
                        dve.wait_ge(o_read, s + 1)
                        if diff_count(s) > 1:
                            dve.wait_ge(o_squared, diff_count(s) - 1)
                        nc.vector.tensor_tensor_reduce(out=obj[0:r, :], in0=ob[0:r, s % 2, :],
                                                       in1=ob[0:r, s % 2, :], scale=1.0, scalar=0.0, op0=ALU.mult,
                                                       op1=ALU.add, accum_out=oss[0:r, s % 2:s % 2 + 1]
                                                       ).then_inc(o_squared, 1)
                topk_at(slot, 3)
                t = tile_at(slot, 13)
                if t is not None:
                    gated(t)
                t = tile_at(slot + 2, 4)
                if t is not None and t >= 2:
                    r, n, o = rows_of(t), nkeys(t), WORK0[t]
                    if t >= 4:
                        dve.wait_ge(qk_done, 16 * (t - 1))
                    nc.vector.tensor_scalar(keep[0:r, t % 2, 0:n], work[0:r, o:o + n], LOW / 2, NEG, ALU.is_gt,
                                            ALU.mult).then_inc(keep_ready, 1)
            def scale2(t):
                r = rows_of(t)
                dve.wait_ge(ld_x2[t % 2], 16 * (t // 2 + 1))
                if t >= 2:
                    for half in range(2):
                        t_wait_full(dve, ("f", t - 2, half))
                dve.wait_ge(x2_rms, t + 1)
                nc.vector.tensor_scalar(x2n[0:r, t % 2, :], x2in[0:r, t % 2, :], mss[0:r, 1, t:t + 1], None, ALU.mult
                                        ).then_inc(x2n_ready, 1)

            def modulate2(t):
                g, r = int(t == 8), rows_of(t)
                if t >= 2:
                    dve.wait_ge(lo2_ready[t % 2], t // 2)
                bank = t_wait_full(dve, ("f", t, 0))
                for k in range(4):
                    last = nc.vector.tensor_scalar(v2[:, t % 2, k, 0:r], bank[:, 128 * k:128 * k + r],
                                                   scaleA[:, 1, k, g:g + 1], modT[:, 24 + k, g:g + 1],
                                                   ALU.mult, ALU.add)
                last.then_inc(freed(("f", t, 0)), 1)

            scale2(0)
            for t in range(NT):
                if t + 1 < NT:
                    scale2(t + 1)
                modulate2(t)
                if t and t % 2 == 0:
                    low_rows(nc.vector, hi2_ready, lo2_ready, h2l, v2, h2h, t - 1)
                if t == TAIL_RESIDUAL:
                    gated(LAST)
            nc.vector.memset(top8[:, 0:1], 0.0).then_inc(hv_ready, 1)
            nc.vector.memset(top8[:, 1:2], 0.0).then_inc(hv_ready, 1)
            for i in range(YBANKS):
                nc.vector.memset(top8[:, 2 + i:3 + i], 0.0).then_inc(y_added, 1)

            def finish(t):
                rows, g = y_rows(t), int(t == 8)
                dve.wait_ge(y_rms, t + 1)
                if t == 0:
                    dve.wait_ge(ld_gate2, 32)
                nc.vector.scalar_tensor_tensor(out=yacc[rows, t, :], in0=yacc[rows, t, :],
                                               scalar=mss[rows, 0, t:t + 1], in1=gate2[rows, g, :],
                                               op0=ALU.mult, op1=ALU.mult).then_inc(y_scaled, 1)

            def ffn_dve(g, last):
                for u in range(6):
                    n = CHUNKS[u % 3][1]
                    dve.wait_ge(silu_out, 6 * g + u + 1)
                    dve.wait_ge(a_lo, 6 * g + u + 1)
                    nc.vector.tensor_tensor(hv[:, u % 2, 0:n], sg[:, u % 2, 0:n], S[u % 2][:, 512:512 + n], ALU.mult
                                            ).then_inc(hv_ready, 1)
                dve.wait_ge(yacc_zero, 1)
                for u in range(18):
                    t, half = divmod(u, 2)
                    dve.wait_ge(y_done, 18 * g + u + 1)
                    at = yacc[:, t, 512 * half:512 * half + 512]
                    nc.vector.tensor_tensor(at, at, YB[u % 3][:, :], ALU.add).then_inc(y_added, 1)

                    if last and half and t:
                        finish(t - 1)

            with dve.Fori(0, FGROUPS - 1) as g:
                ffn_dve(g, False)
            ffn_dve(FGROUPS - 1, True)
            finish(NT - 1)

        @block.tensor
        def _(pe):
            pe.wait_ge(consts, 2)
            pe.wait_ge(ld_params, 16 * len(PARAM_ROWS))
            bank = t_wait_free(pe, ("params",))
            pe.transpose(bank[:, 0:97], prow[:, :], ident[0:97, 0:97]).then_inc(filled(("params",)), 1)

            def ada_products(j):
                pe.wait_ge(ld_ada[ada_slot(j)], 16 * ada_turn(j)[0])
                if j >= 2:
                    pe.wait_ge(ada_out, j - 1)
                for k in range(KB):
                    last = pe.matmul(S[0][0:2, 512 * (j % 2):512 * (j % 2) + ADA_W], csil[:, k, :], ada_in(j)[:, k, :],
                                     start=(k == 0), stop=(k == KB - 1))
                last.then_inc(ada_used, 1)

            def ada_transposes(j):
                pe.wait_ge(ada_out, j + 1)
                for i in range(ADA_W // 128):
                    nb = ADA_W // 128 * j + i
                    out = PJ[1][:, 2 * nb:2 * nb + 2] if j < ADA_FIRST else S[1][:, 2 * (nb - 16):2 * (nb - 16) + 2]
                    last = pe.transpose(out, adarow[:, 128 * i:128 * i + 128], ident[0:2, 0:2])
                last.then_inc(ada_cols, 1)

            def transpose_x(t):
                r = rows_of(t)
                pe.wait_ge(xn_ready, t + 1)
                for half in range(2):
                    bank = t_wait_free(pe, ("x", t, half))
                    for j in range(4):
                        k = 4 * half + j
                        last = pe.transpose(bank[:, 128 * j:128 * j + r], xn[0:r, t % 2, 128 * k:128 * k + 128],
                                            ident[0:r, 0:r])
                    last.then_inc(filled(("x", t, half)), 1)

            pe.wait_ge(silu_done, 1)
            for j in range(ADA_FIRST):
                ada_products(j)
                if j:
                    ada_transposes(j - 1)
            ada_transposes(ADA_FIRST - 1)
            pe.wait_ge(ld_tab, 32)
            for i in range(3):
                if i:
                    pe.wait_ge(r_out, i)
                pe.matmul(PJ[0][0:12, 0:384], tab[:, :], onehot[:, 384 * i:384 * i + 384], start=True, stop=True
                          ).then_inc(r_made, 1)

            def chunk(b, c):
                c0, n = CHUNKS[c]
                i, w = 3 * b + c, BLOCKS[b][3]
                if b == 0:
                    wait_lows(pe, lo_ready, -(-(c0 + n) // 128))
                if c == 0:
                    pe.wait_ge(w_lo, b + 1)
                if i >= 2:
                    pe.wait_ge(chunk_out, i - 1)
                for k in range(KB):
                    for p, (wp, hp) in enumerate(((wh, hTh), (wh, hTl), (wl, hTh))):
                        last = pe.matmul(PJ[i % 2][0:w, 0:n], wp[:, b % 2, k, 0:w], hp[:, k, c0:c0 + n],
                                         start=(k == 0 and p == 0), stop=(k == KB - 1 and p == 2))
                last.then_inc(chunk_done, 1)

            for t in range(NT):
                transpose_x(t)
                if t in EARLY:
                    chunk(0, EARLY[t])
            pe.wait_ge(ld_cache, 96)
            for j in range(3):
                bank = t_wait_free(pe, ("cache", j))
                for m in range(4):
                    i = m % 2
                    if j < 2:
                        h = 2 * j + m // 2
                        last = pe.transpose(bank[:, 128 * m:128 * m + 128], cachek[:, i, 128 * h:128 * h + 128],
                                            ident[:, :])
                    elif m < 2:
                        last = pe.transpose(bank[:, 128 * m:128 * m + 128], cachek[:, i, 512:640], ident[:, :])
                    else:
                        last = pe.transpose(bank[0:64, 128 * m:128 * m + 128], cachek[:, i, 640:704], ident[:, :])
                last.then_inc(filled(("cache", j)), 1)
            for b in range(NB):
                kind, _, _, w = BLOCKS[b]
                t = dots_tile(b)
                if t is not None:
                    r, n, k0 = rows_of(t), nkeys(t), key0(t)
                    if t == 2:
                        pe.wait_ge(chunk_out, 9)
                    for hh in range(NH_I):
                        u = NH_I * (t - 2) + hh
                        part = slice(64 * (hh % 2), 64 * (hh % 2) + 64)
                        if u >= 2:
                            pe.wait_ge(relu_done, u - 1)
                        for o in range(0, n, 512):
                            m = min(512, n - o)
                            last = pe.matmul(S[u % 2][0:r, o:o + m], iqT[part, hh // 2, 128 * t:128 * t + r],
                                             ikD[part, k0 + o:k0 + o + m], start=True, stop=True)
                        last.then_inc(dots_done, 1)
                for c in range(3):
                    if b or c not in EARLY.values():
                        chunk(b, c)
                for j in ada_after(b - 1)[1:]:
                    ada_transposes(j)
                if b - 1 in NATURAL:
                    v = b - 1
                    wv = BLOCKS[v][3]
                    pe.wait_ge(chunk_out, 3 * (v + 1))
                    for q in range(3):
                        bank = t_wait_free(pe, ("nat", v, q))
                        for t in range(4 * q, min(4 * q + 4, NT)):
                            o = 128 * (t - 4 * q)
                            last = pe.transpose(bank[0:rows_of(t), o:o + wv], nat_source(v, t), ident[0:wv, 0:wv])
                        last.then_inc(filled(("nat", v, q)), 1)
                for j in ada_after(b):
                    if j == ADA_FIRST:
                        pe.wait_ge(relu_done, NH_I * len(TOPK_TILES))
                    ada_products(j)
                for j in ada_after(b)[:1]:
                    ada_transposes(j)
            pe.wait_ge(gates_ready, 1)
            bank = t_wait_free(pe, ("gates",))
            pe.transpose(bank[0:32, 0:128], gates[:, :, :, :].rearrange("p a g k -> p (a g k)"), ident[:, :]
                         ).then_inc(filled(("gates",)), 1)
            def transpose_probs(key):
                _, s, m, q = key
                t, _, r, _ = step(s)
                if sparse(s):
                    pe.wait_ge(exp_done, 2 * s + m + 1)
                else:
                    pe.wait_ge(combined, diff_count(s))
                bank = t_wait_free(pe, key)
                for j, (o, w) in enumerate(key_blocks(t)[4 * q:4 * q + 4]):
                    last = pe.transpose(bank[0:w, 128 * j:128 * j + r], sc[0:r, s % 3, m, o:o + w], ident[0:r, 0:r])
                last.then_inc(filled(key), 1)

            def scores(s, m):
                t, i, r, n = step(s)
                k0 = key0(t)
                if i == 0 and m == 0:
                    pe.wait_ge(ld_q[t % 2], 16 * (t // 2 + 1))
                if t == 0 and i == 7 and m == 0:
                    pe.wait_ge(ld_q7, 16)
                if sparse(s) and t >= 2 and i == 4 and m == 0:
                    pe.wait_ge(keep_ready, t - 1)
                part = slice(64 * m, 64 * m + 64)
                if s >= 1:
                    pe.wait_ge(biased, 2 * (s - 1) + m + 1)
                keys = skD[part, (i - 4) // 2, :] if sparse(s) else kT[part, i, :]
                masked = t < 8 or sparse(s)
                for o in range(0, n, 512):
                    w = min(512, n - o)
                    tail = masked and ((sparse(s) and t >= 2) or o + w == n)
                    last = pe.matmul(S[m][0:r, o:o + w], qt[part, t % 2, i, 0:r], keys[:, k0 + o:k0 + o + w],
                                     start=True, stop=not tail)
                    if sparse(s) and t >= 2:
                        last = pe.matmul(S[m][0:r, o:o + w], identb[:, 0:r], keep[:, t % 2, o:o + w],
                                         start=False, stop=True)
                    elif tail:
                        last = pe.matmul(S[m][0:r, n - 128:n], identb[:, :], maskb[:, :], start=False, stop=True)
                last.then_inc(qk_done, 1)

            def out_projection(t, half):
                r = rows_of(t)
                if t == 0 and half == 0:
                    pe.wait_ge(ld_wout, 16 * KB)
                if 2 * t + half:
                    pe.wait_ge(m_out, 2 * t + half)
                for i in range(8 * t, 8 * t + 8):
                    t_wait_freed(pe, ("o", i))
                for k in range(KB):
                    last = pe.matmul(PJ[1][0:r, :], oT[:, t % 2, k, 0:r], wout[:, k, 512 * half:512 * half + 512],
                                     start=(k == 0), stop=(k == KB - 1))
                last.then_inc(m_done, 1)

            for slot in range(SLOTS):
                for m in range(2):
                    for key in prob_part(slot, m):
                        transpose_probs(key)
                    if slot < NSTEPS:
                        scores(slot, m)
                if 3 <= slot < NSTEPS + 3:
                    s = slot - 3
                    r = rows_of(s // 8)
                    if sparse(s):
                        pe.wait_ge(o_read, s + 1)
                    else:
                        pe.wait_ge(o_ready, diff_count(s))
                    bank = t_wait_free(pe, ("o", s))
                    pe.transpose(bank[:, 0:r], ob[0:r, s % 2, :], ident[0:r, 0:r]).then_inc(filled(("o", s)), 1)
                if 2 <= slot < NSTEPS + 2:
                    s = slot - 2
                    t, i, r, n = step(s)
                    blocks = key_blocks(t)
                    for key in prob_groups(s):
                        t_wait_freed(pe, key)
                    if s >= 1:
                        pe.wait_ge(o_read, s)
                    if i == 0 and t < 8:
                        pe.wait_ge(ld_v[t % 2], 32 * (t // 2 + 1))
                    elif i == 0:
                        pe.wait_ge(ld_vfix, 96)
                    for m in range(2 if sparse(s) else 1):
                        out = PJ[0][0:r, 64 * m:64 * m + 64] if sparse(s) else PJ[0][0:r, 0:128]
                        c, e = (512 + 64 * ((i - 4) // 2), 64) if sparse(s) else (128 * i, 128)
                        for j, (o, w) in enumerate(blocks):
                            vt_ = j if t < 8 else 8 + j
                            last = pe.matmul(out, aT[0:w, m, j, 0:r], vsb[0:w, vt_, c:c + e],
                                             start=(j == 0), stop=(j == len(blocks) - 1))
                    last.then_inc(pv_done, 1)
                if out_half(slot):
                    out_projection(*out_half(slot))
            for t in range(NT):
                r = rows_of(t)
                pe.wait_ge(x2n_ready, t + 1)
                for half in range(2):
                    bank = t_wait_free(pe, ("f", t, half))
                    for j in range(4):
                        k = 4 * half + j
                        last = pe.transpose(bank[:, 128 * j:128 * j + r], x2n[0:r, t % 2, 128 * k:128 * k + 128],
                                            ident[0:r, 0:r])
                    last.then_inc(filled(("f", t, half)), 1)
                if t in TAIL_OUT:
                    out_projection(LAST, TAIL_OUT[t])

            def ffn_pe(g, first=False):
                for u in range(6):
                    slot, c = divmod(u, 3)
                    c0, n = CHUNKS[c]
                    if first and slot == 0:
                        wait_lows(pe, lo2_ready, -(-(c0 + n) // 128))
                    if c == 0:
                        pe.wait_ge(g_lo, 2 * g + slot + 1)
                    pe.wait_ge(hv_ready, 6 * g + u + 1)
                    for part in range(2):
                        for k in range(KB):
                            for p, (wp, hp) in enumerate(((gh, h2h), (gh, h2l), (gl, h2h))):
                                last = pe.matmul(S[u % 2][:, 512 * part:512 * part + n],
                                                 wp[:, slot, k, 128 * part:128 * part + 128], hp[:, k, c0:c0 + n],
                                                 start=(k == 0 and p == 0), stop=(k == KB - 1 and p == 2))
                    last.then_inc(gu_done, 1)
                pe.wait_ge(d_lo, 2 * g + 2)
                for u in range(18):
                    t, half = divmod(u, 2)
                    if half == 0:
                        c = next(i for i, (c0, n) in enumerate(CHUNKS) if y_cols(t).stop <= c0 + n)
                        pe.wait_ge(a_lo, PAIRS + 6 * g + 4 + c)
                    pe.wait_ge(y_added, 18 * g + u + 1)
                    for b in range(2):
                        for p, (ap, wp) in enumerate(((ah, dh), (ah, dl), (al, dh))):
                            last = pe.matmul(YB[u % 3][:, :], ap[:, b, y_cols(t)],
                                             wp[:, b, 512 * half:512 * half + 512],
                                             start=(b == 0 and p == 0), stop=(b == 1 and p == 2))
                    last.then_inc(y_done, 1)

            ffn_pe(0, True)
            with pe.Fori(1, FGROUPS - 1) as g:
                ffn_pe(g)
            ffn_pe(FGROUPS - 1)


def arena_offset(nc, arena):
    return nc.sbuf_base - ARENA if isinstance(nc.sbuf_base, int) else nc.sbuf_base() - ARENA


QBLOCKS_POS = {b: (BLOCKS[b][1] if BLOCKS[b][0] == "dq" else 4 + BLOCKS[b][1]) for b in QBLOCKS}
PARAM_ROWS = [("c_p", 0, 8), ("c_s", 8, 8), ("g_pre_mix", 16, 8), ("g_pre_ffn", 24, 8), ("g_post_mix", 32, 8),
              ("g_post_ffn", 40, 8), ("b_ada", 48, 48), ("g_subln", 96, 1)]

INPUTS = [("x_p", "x_prompt", (SEQ, D)), ("x_s", "x_sample", (DEC, D)),
          ("c_dk", "cache_diff_k", (PAST, 4, 128)), ("c_dv", "cache_diff_v", (PAST, 4, 128)),
          ("c_sk", "cache_dsa_k", (PAST, 2, 64)), ("c_sv", "cache_dsa_v", (PAST, 2, 64)),
          ("c_ik", "cache_dsa_kidx", (PAST, 64)), ("c_p", "c_prompt", (D,)), ("c_s", "c_sample", (D,)),
          ("w_ada", "w_ada", (D, 6 * D)), ("b_ada", "b_ada", (6 * D,)), ("g_pre_mix", "g_pre_mix", (D,)),
          ("g_post_mix", "g_post_mix", (D,)), ("g_pre_ffn", "g_pre_ffn", (D,)), ("g_post_ffn", "g_post_ffn", (D,)),
          ("w_in", "w_in", (D, 2628)), ("lq1", "lambda_q1", (DH,)), ("lk1", "lambda_k1", (DH,)),
          ("lq2", "lambda_q2", (DH,)), ("lk2", "lambda_k2", (DH,)), ("g_subln", "g_subln", (128,)),
          ("w_out", "w_out", (D, D)), ("w_gu", "w_gate_up", (D, 2 * FF)), ("w_down", "w_down", (FF, D)),
          ("tab", "rel_bias_table", (BUCKETS, 12))]
OUTPUTS = [("y_p", (SEQ, D), (1, SEQ, D)), ("y_s", (DEC, D), (1, DEC, D)),
           ("dk_p", (SEQ, 4, 128), (1, 1, SEQ, 4, 128)), ("dv_p", (SEQ, 4, 128), (1, 1, SEQ, 4, 128)),
           ("sk_p", (SEQ, 128), (1, 1, SEQ, 2, 64)), ("sv_p", (SEQ, 128), (1, 1, SEQ, 2, 64)),
           ("ik_p", (SEQ, 64), (1, 1, SEQ, 64)),
           ("dk_s", (DEC, 4, 128), (1, 1, DEC, 4, 128)), ("dv_s", (DEC, 4, 128), (1, 1, DEC, 4, 128)),
           ("sk_s", (DEC, 128), (1, 1, DEC, 2, 64)), ("sv_s", (DEC, 128), (1, 1, DEC, 2, 64)),
           ("ik_s", (DEC, 64), (1, 1, DEC, 64))]


def kernel(**inputs):
    import concourse.bacc as bacc
    from concourse.bass_utils import run_bass_kernel_spmd

    nc = bacc.Bacc("TRN2", target_bir_lowering=False, num_devices=1)
    arrays, I, O = {}, {}, {}
    for name, arg, shape in INPUTS:
        arrays["in_" + name] = np.ascontiguousarray(inputs[arg]).reshape(shape)
        I[name] = nc.dram_tensor("in_" + name, shape, F32, kind="ExternalInput").ap()
    arrays["in_onehot"] = bias_row_onehot()
    I["onehot"] = nc.dram_tensor("in_onehot", (BUCKETS, NREL), F32, kind="ExternalInput").ap()
    for name, shape, _ in OUTPUTS:
        O[name] = nc.dram_tensor("out_" + name, shape, F32, kind="ExternalOutput").ap()
    build(nc, I, O)
    got = run_bass_kernel_spmd(nc, [arrays], core_ids=[0]).results[0]
    return tuple(got["out_" + name].reshape(shape) for name, _, shape in OUTPUTS)
```
